# Optimizing a Trainium2 kernel written in Bass

```python
import math
import jax, jax.numpy as jnp
from jax import lax
import numpy as np

D_MODEL = 1024
BATCH = 1
SEQ = 1024
DEPTH = 1

HEAD_DIM = 64
SWA_Q_HEADS = 8
SWA_KV_HEADS = 2
SWA_WINDOW = 128
DIL_HEADS = 4
DIL_PAIRS = ((128, 1), (512, 4), (2048, 16))
MEM_HEADS = 4
MEM_LEN = 256

BLOCK = 128
ROPE_THETA = 10000.0
LN_EPS = 1e-5
RMS_EPS = 1e-6
DEEPNORM_ALPHA = (2 * DEPTH) ** 0.25
DEEPNORM_BETA = (8 * DEPTH) ** -0.25

W_A = SWA_Q_HEADS * HEAD_DIM
W_KV_A = SWA_KV_HEADS * HEAD_DIM
W_B = DIL_HEADS * HEAD_DIM
W_C = MEM_HEADS * HEAD_DIM
D_MIX = W_A + W_B + W_C
IN_SPLITS = (W_A, W_KV_A, W_KV_A, W_B, W_B, W_B, W_C, D_MIX)
D_IN = sum(IN_SPLITS)

kernel_name = "hymba_swa_sink_dilated_mem_deepnorm"

def rope_tables(seq_len):
    pos = jnp.arange(seq_len, dtype=jnp.float32)
    inv = ROPE_THETA ** (-jnp.arange(0, HEAD_DIM, 2, dtype=jnp.float32) / HEAD_DIM)
    ang = pos[:, None] * inv[None, :]
    ang = jnp.concatenate([ang, ang], axis=-1)
    return jnp.cos(ang), jnp.sin(ang)

def apply_rope(t, cos, sin):
    tf = t.astype(jnp.float32)
    half = HEAD_DIM // 2
    rot = jnp.concatenate([-tf[..., half:], tf[..., :half]], axis=-1)
    return (tf * cos[None, :, None, :] + rot * sin[None, :, None, :]).astype(t.dtype)

def banded_causal_attention(q, k, v, max_dist, sinks=None):
    N, L, H, D = q.shape
    Hkv = k.shape[2]
    G = H // Hkv
    n_blk = -(-L // BLOCK)
    pad = n_blk * BLOCK - L
    if pad:
        q, k, v = [jnp.pad(t, ((0, 0), (0, pad), (0, 0), (0, 0))) for t in (q, k, v)]
    qb = q.reshape(N, n_blk, BLOCK, Hkv, G, D)
    kb = k.reshape(N, n_blk, BLOCK, Hkv, D)
    vb = v.reshape(N, n_blk, BLOCK, Hkv, D)

    def with_prev(t):
        prev = jnp.pad(t, ((0, 0), (1, 0), (0, 0), (0, 0), (0, 0)))[:, :-1]
        return jnp.concatenate([prev, t], axis=2)

    kk, vv = with_prev(kb), with_prev(vb)
    s = jnp.einsum('nbqhgd,nbkhd->nbhgqk', qb, kk,
                   preferred_element_type=jnp.float32) * (D ** -0.5)
    qi = jnp.arange(BLOCK)[:, None]
    kj = jnp.arange(2 * BLOCK)[None, :]
    dist = qi + BLOCK - kj
    band = (dist >= 0) & (dist <= max_dist)
    blk = jnp.arange(n_blk)[:, None, None]
    mask = band[None] & ((blk > 0) | (kj >= BLOCK)[None])
    s = jnp.where(mask[None, :, None, None], s, -jnp.inf)
    m = s.max(axis=-1)
    if sinks is not None:
        sink = sinks.astype(jnp.float32).reshape(Hkv, G)[None, None, :, :, None]
        m = jnp.maximum(m, sink)
    p = jnp.exp(s - m[..., None])
    denom = p.sum(axis=-1)
    if sinks is not None:
        denom = denom + jnp.exp(sink - m)
    o = jnp.einsum('nbhgqk,nbkhd->nbqhgd', (p / denom[..., None]).astype(v.dtype), vv)
    lse = m + jnp.log(denom)
    o = o.reshape(N, n_blk * BLOCK, H, D)[:, :L]
    lse = lse.transpose(0, 1, 4, 2, 3).reshape(N, n_blk * BLOCK, H)[:, :L]
    return o, lse

def dilated_attention(q, k, v):
    B, S, H, D = q.shape
    outs, lses = [], []
    for window, dil in DIL_PAIRS:
        Ls = S // dil

        def to_stream(t):
            return t.reshape(B, Ls, dil, H, D).transpose(0, 2, 1, 3, 4).reshape(B * dil, Ls, H, D)

        o, lse = banded_causal_attention(to_stream(q), to_stream(k), to_stream(v), window // dil)
        outs.append(o.reshape(B, dil, Ls, H, D).transpose(0, 2, 1, 3, 4).reshape(B, S, H, D))
        lses.append(lse.reshape(B, dil, Ls, H).transpose(0, 2, 1, 3).reshape(B, S, H))
    w = jax.nn.softmax(jnp.stack(lses), axis=0)
    o = jnp.einsum('pbsh,pbshd->bshd', w, jnp.stack(outs).astype(jnp.float32))
    return o.astype(q.dtype)

def memory_attention(q, mk, mv):
    s = jnp.einsum('bshd,bmhd->bhsm', q, mk, preferred_element_type=jnp.float32) * (HEAD_DIM ** -0.5)
    p = jax.nn.softmax(s, axis=-1)
    return jnp.einsum('bhsm,bmhd->bshd', p.astype(mv.dtype), mv)

def rms_normalize(t):
    tf = t.astype(jnp.float32)
    return tf * lax.rsqrt(jnp.mean(tf * tf, axis=-1, keepdims=True) + RMS_EPS)

def layer_norm(t, gain, bias):
    tf = t.astype(jnp.float32)
    mu = jnp.mean(tf, axis=-1, keepdims=True)
    var = jnp.mean(jnp.square(tf - mu), axis=-1, keepdims=True)
    return (tf - mu) * lax.rsqrt(var + LN_EPS) * gain.astype(jnp.float32) + bias.astype(jnp.float32)

def setup_inputs(seed: int = 0) -> dict:
    key = jax.random.key(seed)
    ks = jax.random.split(key, 10)
    x = jax.random.normal(ks[0], (BATCH, SEQ, D_MODEL), jnp.float32)
    mem = jax.random.normal(ks[1], (BATCH, MEM_LEN, D_MODEL), jnp.float32)
    w_in = jax.random.normal(ks[2], (DEPTH, D_MODEL, D_IN), jnp.float32) * D_MODEL ** -0.5
    b_in = 0.02 * jax.random.normal(ks[3], (DEPTH, D_IN), jnp.float32)
    w_mem = jax.random.normal(ks[4], (DEPTH, D_MODEL, 2 * W_C), jnp.float32) * D_MODEL ** -0.5
    attn_sinks = 0.5 * jax.random.normal(ks[5], (DEPTH, SWA_Q_HEADS), jnp.float32)
    g_branch = 1.0 + 0.05 * jax.random.normal(ks[6], (DEPTH, D_MIX), jnp.float32)
    w_out = (jax.random.normal(ks[7], (DEPTH, D_MIX, D_MODEL), jnp.float32)
             * D_MIX ** -0.5 * DEEPNORM_BETA)
    ln_gain = 1.0 + 0.05 * jax.random.normal(ks[8], (DEPTH, D_MODEL), jnp.float32)
    ln_bias = 0.02 * jax.random.normal(ks[9], (DEPTH, D_MODEL), jnp.float32)
    return {"x": x, "mem": mem, "w_in": w_in, "b_in": b_in, "w_mem": w_mem,
            "attn_sinks": attn_sinks, "g_branch": g_branch, "w_out": w_out,
            "ln_gain": ln_gain, "ln_bias": ln_bias}

def reference(x, mem, w_in, b_in, w_mem, attn_sinks, g_branch, w_out, ln_gain, ln_bias):
    B, S, _ = x.shape
    M = mem.shape[1]
    cos, sin = rope_tables(S)
    split_idx = [int(i) for i in np.cumsum(IN_SPLITS)[:-1]]

    def heads(t, n):
        return t.reshape(t.shape[0], t.shape[1], n, HEAD_DIM)

    for l in range(DEPTH):
        h = jnp.einsum('bsd,de->bse', x, w_in[l]) + b_in[l]
        qa, ka, va, qb, kb, vb, qc, z = jnp.split(h, split_idx, axis=-1)

        oa, _ = banded_causal_attention(apply_rope(heads(qa, SWA_Q_HEADS), cos, sin),
                                        apply_rope(heads(ka, SWA_KV_HEADS), cos, sin),
                                        heads(va, SWA_KV_HEADS),
                                        SWA_WINDOW - 1, attn_sinks[l])
        ob = dilated_attention(apply_rope(heads(qb, DIL_HEADS), cos, sin),
                               apply_rope(heads(kb, DIL_HEADS), cos, sin),
                               heads(vb, DIL_HEADS))
        mkv = jnp.einsum('bmd,de->bme', mem, w_mem[l])
        mk, mv = jnp.split(mkv, 2, axis=-1)
        oc = memory_attention(heads(qc, MEM_HEADS), heads(mk, MEM_HEADS), heads(mv, MEM_HEADS))

        y = jnp.concatenate([rms_normalize(oa.reshape(B, S, W_A)),
                             rms_normalize(ob.reshape(B, S, W_B)),
                             rms_normalize(oc.reshape(B, S, W_C))], axis=-1)
        y = y * g_branch[l].astype(jnp.float32) * jax.nn.silu(z.astype(jnp.float32))
        y = jnp.einsum('bse,ed->bsd', y.astype(x.dtype), w_out[l])

        x = layer_norm(DEEPNORM_ALPHA * x + y, ln_gain[l], ln_bias[l]).astype(x.dtype)
    return x


_drawn_inputs = setup_inputs


def setup_inputs(seed=0):
    import zlib

    import numpy as np

    out = dict(_drawn_inputs(seed))
    spreads = {}
    factors = {'attn_sinks': 8.0, 'g_branch': 3.866, 'ln_bias': 2.858}
    for name, (base, spread) in spreads.items():
        noise = np.random.default_rng([zlib.crc32(name.encode()), seed]).standard_normal(out[name].shape)
        drawn = base * np.exp(spread * noise) if base else spread * noise
        out[name] = __import__('jax').numpy.asarray(drawn.astype(out[name].dtype))
    for name, factor in factors.items():
        out[name] = (out[name] * factor).astype(out[name].dtype)
    return out
```

```python
from contextlib import ExitStack

import numpy as np

import concourse.bass as bass
from concourse import mybir

F32 = mybir.dt.float32
F32R = mybir.dt.float32r
ALU = mybir.AluOpType
ACT = mybir.ActivationFunctionType
AX = mybir.AxisListType

P = 128
SEQ = 1024
DM = 1024
MEM = 256
NB = SEQ // P
NBM = MEM // P
KT = DM // P
HD = 64
HA, GA = 8, 2
HB = 4
HC = 4
WINDOW = 128
PAIRS = ((128, 1), (512, 4), (2048, 16))
DEPTH = 1
ALPHA = float((2 * DEPTH) ** 0.25)
RMS_EPS = 1e-6
LN_EPS = 1e-5
SCALE = HD ** -0.5
MASKED = -1e30
C = 256
HALF = 512

W_A, W_KV, W_B, W_C = HA * HD, GA * HD, HB * HD, HC * HD
COL_QA, COL_KA, COL_VA = 0, W_A, W_A + W_KV
COL_QB = COL_VA + W_KV
COL_KB, COL_VB = COL_QB + W_B, COL_QB + 2 * W_B
COL_QC = COL_VB + W_B
COL_Z = COL_QC + W_C
QKV = COL_Z
FT = (W_A + W_B + W_C) // P


def chunks():
    return [("mk", True, 0, None), ("mv", True, W_C, None),
            ("kva", False, COL_KA, None), ("kb", False, COL_KB, None), ("vb", False, COL_VB, None),
            ("q", False, COL_QA, 0), ("q", False, COL_QA + C, C), ("q", False, COL_QB, W_A),
            ("qc", False, COL_QC, W_A + W_B)]


def units():
    out = []
    for i in range(NB):
        window = min(i + 1, 2)
        a = [("a", i, 2 * j, 2, window) for j in range(HA // 2)]
        b = [("b", i, j, 1, i + 1) for j in range(HB)]
        c = [("c", i, 2 * j, 2, NBM) for j in range(HC // 2)]
        out += [a[0], b[0], a[1], b[1], a[2], b[2], a[3], b[3], c[0], c[1]]
    return out


UNITS = units()
UB = len(UNITS) // NB
AT_RMS, AT_SCALE, AT_Y, AT_YSPLIT, AT_OUT = UB + 3, UB + 4, UB + 5, UB + 6, UB + 7
AT_RES0, AT_RES1 = AT_OUT + 5, AT_OUT + 10
AT_STATS, AT_NORM = AT_OUT + 11, AT_OUT + 12
ITERATIONS = UB * (NB - 1) + AT_NORM + 1
WO_FIRST = 5
PIECES = 10


def block_at(v, at):
    i, r = divmod(v - at, UB)
    return i if r == 0 and 0 <= i < NB else None


def key_chunks(u):
    kind, _, _, heads, nk = UNITS[u]
    if kind != "b":
        return [(0, C * (heads - 1) + nk * P)]
    return [(c, min(c + HALF, nk * P)) for c in range(0, nk * P, HALF)]


def prob_tiles(u):
    kind, i, _, heads, nk = UNITS[u]
    if kind == "b":
        return [(0, t, t * P) for t in range(nk)]
    first = i + 1 - nk if kind == "a" else 0
    return [(hh, first + t, hh * C + t * P) for hh in range(heads) for t in range(nk)]


class Plan:

    def __init__(self):
        self.chunks = chunks()
        self.jobs = [(c, i) for c, (_, of_mem, _, _) in enumerate(self.chunks)
                     for i in range(NBM if of_mem else NB)]
        self.last_job = {c: max(n for n, j in enumerate(self.jobs) if j[0] == c)
                         for c in range(len(self.chunks))}
        self.key_jobs = [n for n, (c, _) in enumerate(self.jobs)
                         if self.chunks[c][0] in ("mk", "kva", "kb")]
        self.steps = [("rows", 0), ("rows", 1), ("rows", 2)]
        for n in range(len(self.jobs)):
            if n and n + 2 < NBM + NB:
                self.steps.append(("rows", n + 2))
            self.steps.append(("job", n))
            if n - 1 in self.key_jobs:
                self.steps.append(("keys", self.key_jobs.index(n - 1)))
        wide, narrow = [], []
        for what, n in self.steps:
            if what == "rows":
                narrow += [("rows", n, h) for h in range(2)]
            else:
                (narrow if what == "keys" else wide).append((what, n))
        wide += [("gate", n) for n in range(2 * FT)]
        self.pt_unit = []
        self.pt = {}
        for v in range(ITERATIONS):
            if v < len(UNITS):
                narrow.append(("q", v))
            if 0 <= v - 1 < len(UNITS):
                wide += [("scores", v - 1, c) for c in range(len(key_chunks(v - 1)))]
            if 0 <= v - 2 < len(UNITS):
                for c in range(-(-len(prob_tiles(v - 2)) // 4)):
                    self.pt[v - 2, c] = len(self.pt_unit)
                    self.pt_unit.append(v - 2)
                    narrow.append(("probs", v - 2, c))
            if block_at(v, AT_Y) is not None:
                narrow += [("y", block_at(v, AT_Y), h) for h in range(2)]
        self.wide = {key: n for n, key in enumerate(wide)}
        self.narrow = {key: n for n, key in enumerate(narrow)}
        for n, key in enumerate(wide):
            assert key[0] != "scores" or wide[n - 3][0] == "gate" or wide[n - 3][1] <= key[1] - 2

    def pt_chunks(self, u):
        return [(c, self.pt[u, c]) for c in range(-(-len(prob_tiles(u)) // 4))]


def layer(nc, x, mem, w_in, b_in, w_mem, sinks, g_branch, w_out, ln_gain, ln_bias,
          ident_d, rope_d, mask_a_d, mask_b_d, out):
    plan = Plan()
    jobs, kinds = plan.jobs, plan.chunks
    n_jobs, n_units = len(jobs), len(UNITS)

    with ExitStack() as ctx:
        def sem(name):
            return ctx.enter_context(nc.semaphore(name))

        ident_in, bias_in, rope_in = sem("ident_in"), sem("bias_in"), sem("rope_in")
        gate_cols_in, sinks_in, masks_in = sem("gate_cols_in"), sem("sinks_in"), sem("masks_in")
        wo_in, ln_in = sem("wo_in"), sem("ln_in")
        rows_in = [sem(f"rows_in{s}") for s in range(2)]
        chunk_in = [[sem(f"chunk_in{s}{h}") for h in range(2)] for s in range(3)]
        gate_in = [sem(f"gate_in{s}") for s in range(2)]
        res_in = [sem(f"res_in{s}") for s in range(2)]
        stored = [sem(f"stored{s}") for s in range(2)]
        wide_full, narrow_full = sem("wide_full"), sem("narrow_full")
        narrow_read = [sem(f"narrow_read{b}") for b in range(2)]
        rows_rounded, chunk_rounded, chunk_split = sem("rows_rounded"), sem("chunk_rounded"), sem("chunk_split")
        gate_rounded, gate_split, h_read = sem("gate_rounded"), sem("gate_split"), sem("h_read")
        rope_parts, keys_rotated, q_rotated = sem("rope_parts"), sem("keys_rotated"), sem("q_rotated")
        keys_rounded, negated, gate_exp = sem("keys_rounded"), sem("negated"), sem("gate_exp")
        gate_plus_one, gate_inverted, gate_done = sem("gate_plus_one"), sem("gate_inverted"), sem("gate_done")
        q_twice, q_rounded, row_max = sem("q_twice"), sem("q_rounded"), sem("row_max")
        neg_max, sink_gap_ready, sink_exp_ready = sem("neg_max"), sem("sink_gap_ready"), sem("sink_exp_ready")
        probs_ready, pv_done, den_sum = sem("probs_ready"), sem("pv_done"), sem("den_sum")
        den_rcp, o_done = sem("den_rcp"), sem("o_done")
        squares, rms_logged, rms_ready = sem("squares"), sem("rms_logged"), sem("rms_ready")
        o_scaled, y_rounded, y_split = sem("o_scaled"), sem("y_rounded"), sem("y_split")
        wo_rounded, wo_split, out_full = sem("wo_rounded"), sem("wo_split"), sem("out_full")
        res_sum, ln_part, ln_stats = sem("res_sum"), sem("ln_part"), sem("ln_stats")
        ln_logged, ln_rstd_ready, ln_shift_ready = sem("ln_logged"), sem("ln_rstd_ready"), sem("ln_shift_ready")
        normed, gained, finished = sem("normed"), sem("gained"), sem("finished")

        top = -(-nc.sbuf_base // 32) * 32

        def at(name, shape, dt, offset):
            return nc.alloc_sbuf_tensor_at(name, shape, dt, offset=offset)

        class Region:
            def __init__(self, size):
                nonlocal top
                self.base, top = top, top + size
                self.end = top

        def nbytes(*shape):
            return 4 * int(np.prod(shape))

        r_x = Region(2 * nbytes(KT, SEQ))
        lo_half = r_x.base + nbytes(KT, SEQ)
        x_hi = at("x_hi", [P, KT, SEQ], F32R, r_x.base)
        x_lo = at("x_lo", [P, KT, SEQ], F32R, lo_half)
        wo_hi = at("wo_hi", [P, FT, DM], F32R, r_x.base)
        wo_raw = at("wo_raw", [P, FT, DM], F32, lo_half)
        wo_lo = at("wo_lo", [P, FT, DM], F32R, lo_half)
        r_q = Region(nbytes(NB, DM))
        qo = at("qo", [P, NB, DM], F32, r_q.base)
        y_hi = at("y_hi", [P, NB, FT, P], F32R, r_q.base)
        rows = [at(f"rows{s}", [P, DM], F32, r_q.base + s * nbytes(DM)) for s in range(2)]
        mem_hi = at("mem_hi", [P, KT, MEM], F32R, r_q.base + nbytes(4, DM))
        mem_lo = at("mem_lo", [P, KT, MEM], F32R, r_q.base + nbytes(6, DM))
        k_a = at("k_a", [P, GA, SEQ], F32R, Region(nbytes(GA, SEQ)).base)
        k_b = at("k_b", [P, HB, SEQ], F32R, Region(nbytes(HB, SEQ)).base)
        k_c = at("k_c", [P, HC, MEM], F32R, Region(nbytes(HC, MEM)).base)
        v_a = at("v_a", [P, NB, W_KV], F32, Region(nbytes(NB, W_KV)).base)
        v_b = at("v_b", [P, NB, W_B], F32, Region(nbytes(NB, W_B)).base)
        v_c = at("v_c", [P, NBM, W_C], F32, Region(nbytes(NBM, W_C)).base)
        r_z = Region(nbytes(FT, SEQ))
        zt = at("zt", [P, FT, SEQ], F32, r_z.base)
        y_lo = at("y_lo", [P, FT, SEQ], F32R, r_z.base)
        r_s = Region(4 * nbytes(DM))
        slot = [r_z.base, r_z.base + 2 * nbytes(KT, C), r_s.base]
        w_hi = [at(f"w_hi{s}", [P, KT, C], F32R, o) for s, o in enumerate(slot)]
        w_raw = [at(f"w_raw{s}", [P, KT, C], F32, o + nbytes(KT, C)) for s, o in enumerate(slot)]
        w_lo = [at(f"w_lo{s}", [P, KT, C], F32R, o + nbytes(KT, C)) for s, o in enumerate(slot)]
        gate = [r_s.base + s * 2 * nbytes(KT, P) for s in range(2)]
        g_hi = [at(f"g_hi{s}", [P, KT, P], F32R, o) for s, o in enumerate(gate)]
        g_raw = [at(f"g_raw{s}", [P, KT, P], F32, o + nbytes(KT, P)) for s, o in enumerate(gate)]
        g_lo = [at(f"g_lo{s}", [P, KT, P], F32R, o + nbytes(KT, P)) for s, o in enumerate(gate)]
        gain = at("gain", [P, DM], F32, r_s.base)
        bias = at("bias", [P, DM], F32, r_s.base + nbytes(DM))
        res = [at(f"res{s}", [P, DM], F32, r_s.base + (2 + s) * nbytes(DM)) for s in range(2)]
        r_t = Region(nbytes(QKV + 7 * C))
        b_row = at("b_row", [P, QKV], F32, r_t.base)
        h_at = r_t.base + nbytes(QKV)
        h_sb = at("h_sb", [P, C], F32, h_at)
        rot_cos = at("rot_cos", [P, C], F32, h_at + nbytes(C))
        rot_sin = at("rot_sin", [P, C], F32, h_at + 2 * nbytes(C))
        keys2 = [at(f"keys2{s}", [P, C // HD, 2, HD], F32, h_at + (3 + 2 * s) * nbytes(C)) for s in range(2)]
        prob = [at(f"prob{s}", [P, SEQ], F32, r_t.base + s * nbytes(SEQ)) for s in range(2)]
        q_at = r_t.base + 2 * nbytes(SEQ)
        q_hi = [at(f"q_hi{s}", [P, 2 * P], F32R, q_at + s * nbytes(2 * P)) for s in range(2)]
        q_lo = [at(f"q_lo{s}", [P, 2 * P], F32R, q_at + (2 + s) * nbytes(2 * P)) for s in range(2)]
        r_r = Region(nbytes(NB, 2 * HD))
        q2_at = q_at + 4 * nbytes(2 * P)
        q2 = [at(f"q2{s}", [P, 2, 2, HD], F32, q2_at + s * nbytes(2 * P)) for s in range(2)]
        rope = at("rope", [P, NB, 2 * HD], F32, r_r.base)
        gate_e = [at(f"gate_e{s}", [P, HALF], F32, Region(nbytes(HALF)).base) for s in range(2)]
        pt_at = [r_r.base, r_r.base + nbytes(HALF), Region(nbytes(HALF)).base, Region(nbytes(HALF)).base]
        prob_t = [at(f"prob_t{s}", [P, HALF], F32, o) for s, o in enumerate(pt_at)]
        mask_a = at("mask_a", [P, 2 * P], F32, Region(nbytes(2 * P)).base)
        mask_b = at("mask_b", [P, SEQ], F32, Region(nbytes(SEQ)).base)
        ident = at("ident", [P, P], F32, Region(nbytes(P)).base)

        def small(name, *shape):
            return at(name, [P, *shape], F32, Region(-(-nbytes(*shape) // 32) * 32).base)

        z_bias, neg_z_bias = small("z_bias", FT), small("neg_z_bias", FT)
        g_col = small("g_col", FT)
        sink_row, neg_sink = small("sink_row", HA), small("neg_sink", HA)
        mx = small("mx", 2, 2)
        nb = small("nb", 4, 2)
        gap, gap_exp = small("gap", 4, 2), small("gap_exp", 4, 2)
        den, den_all, rden = small("den", 4, 2), small("den_all", 4, 2), small("rden", 4, 2)
        sq = small("sq", 2, 3)
        rms_log, rms = small("rms_log", 2, 3), small("rms", 2, 3)
        square_out = at("square_out", [P, DM], mybir.dt.bfloat16, Region(2 * DM).base)
        stats, moments = small("stats", 2, 2, 6), small("moments", 2, 2)
        ln_log, ln_rstd, ln_shift = small("ln_log", 2), small("ln_rstd", 2), small("ln_shift", 2)
        assert top <= nc.sbuf_usable_end, top

        wide = [ctx.enter_context(nc.psum_tensor(f"wide{b}", [P, HALF], F32)) for b in range(3)]
        narrow = [ctx.enter_context(nc.psum_tensor(f"narrow{b}", [P, HALF], F32)) for b in range(2)]
        o_ps = [ctx.enter_context(nc.psum_tensor(f"o_ps{b}", [P, HALF], F32)) for b in range(2)]
        out_ps = ctx.enter_context(nc.psum_tensor("out_ps", [P, HALF], F32))

        def f32(ap):
            return ap.bitcast(F32)

        def bank_of(ring, turns, key):
            n = turns[key]
            return n, ring[n % len(ring)]

        def slot_of(c):
            return (c + 2) % 3

        def heads_view(ap, n):
            return ap.rearrange("p (h d) -> p h d", h=n)

        def key_dst(k):
            c, i = jobs[plan.key_jobs[k]]
            t, n = {"mk": (k_c, HC), "kva": (k_a, GA), "kb": (k_b, HB)}[kinds[c][0]]
            return t[:, :, i * P:(i + 1) * P], n

        def v_tile(u, t, hh):
            kind, _, h0, _, _ = UNITS[u]
            h = h0 + hh
            if kind == "a":
                g = h // (HA // GA)
                return v_a[:, t, g * HD:(g + 1) * HD]
            return (v_b if kind == "b" else v_c)[:, t, h * HD:(h + 1) * HD]

        def q_cols(u, hh):
            kind, _, h0, _, _ = UNITS[u]
            return {"a": 0, "b": W_A, "c": W_A + W_B}[kind] + (h0 + hh) * HD

        a_index = {}
        masked_index = {}
        for u, unit in enumerate(UNITS):
            if unit[0] == "a":
                a_index[u] = len(a_index)
            if unit[0] != "c":
                masked_index[u] = len(masked_index)

        def scores_turn(u):
            return plan.wide["scores", u, len(key_chunks(u)) - 1]

        def probs_turn(u):
            return plan.narrow["probs", u, plan.pt_chunks(u)[-1][0]]

        block = ctx.enter_context(nc.Block())

        @block.sync
        def _(sp):
            def load_rows(r):
                if r >= 2:
                    sp.wait_ge(narrow_full, plan.narrow["rows", r - 2, 1] + 1)
                src = mem[0, r * P:(r + 1) * P, :] if r < NBM else \
                    x[0, (r - NBM) * P:(r - NBM + 1) * P, :]
                sp.dma_start(rows[r % 2][:, :], src).then_inc(rows_in[r % 2], 16)

            def load_chunk(c):
                if c >= 3:
                    sp.wait_ge(wide_full, plan.wide["job", plan.last_job[c - 3]] + 1)
                _, of_mem, col, _ = kinds[c]
                src = (w_mem if of_mem else w_in)[0, :, col:col + C]
                src = src.rearrange("(k p) n -> p k n", p=P)
                for h in range(2):
                    k = slice(h * KT // 2, (h + 1) * KT // 2)
                    sp.dma_start(w_raw[slot_of(c)][:, k, :], src[:, k, :])\
                      .then_inc(chunk_in[slot_of(c)][h], 16)

            def load_gate(f):
                if f < 2:
                    sp.wait_ge(wide_full, plan.wide["job", plan.last_job[6]] + 1)
                else:
                    sp.wait_ge(wide_full, plan.wide["gate", 2 * (f - 2) + 1] + 1)
                src = w_in[0, :, COL_Z + f * P:COL_Z + (f + 1) * P]
                sp.dma_start(g_raw[f % 2][:, :, :], src.rearrange("(k p) n -> p k n", p=P))\
                  .then_inc(gate_in[f % 2], 16)

            load_rows(0)
            sp.dma_start(ident[:, :], ident_d).then_inc(ident_in, 16)
            load_chunk(0)
            load_rows(1)
            load_chunk(1)
            load_rows(2)
            load_chunk(2)
            load_rows(3)
            sp.dma_start(b_row[:, :], b_in[0, 0:QKV].partition_broadcast(P)).then_inc(bias_in, 16)
            load_rows(4)
            sp.dma_start(rope[:, :, :], rope_d.rearrange("(b p) d -> p b d", p=P)).then_inc(rope_in, 16)
            load_rows(5)
            load_rows(6)
            load_chunk(3)
            for r in range(7, NBM + NB):
                load_rows(r)
            with nc.allow_non_contiguous_dma(reason="one value per partition"):
                sp.dma_start(z_bias[:, :], b_in[0, COL_Z:].rearrange("(f p) -> p f", p=P))\
                  .then_inc(gate_cols_in, 16)
                sp.dma_start(g_col[:, :], g_branch[0].rearrange("(f p) -> p f", p=P))\
                  .then_inc(gate_cols_in, 16)
            sp.dma_start(sink_row[:, :], sinks[0].partition_broadcast(P)).then_inc(sinks_in, 16)
            sp.dma_start(mask_a[:, :], mask_a_d).then_inc(masks_in, 16)
            sp.dma_start(mask_b[:, :], mask_b_d).then_inc(masks_in, 16)
            for c in range(4, len(kinds)):
                load_chunk(c)
            for f in range(FT):
                load_gate(f)
            sp.wait_ge(wide_full, plan.wide["gate", 2 * FT - 1] + 1)
            sp.dma_start(wo_raw[:, :, :], w_out[0].rearrange("(k p) n -> p k n", p=P)).then_inc(wo_in, 16)
            sp.dma_start(gain[:, :], ln_gain[0].partition_broadcast(P)).then_inc(ln_in, 16)
            sp.dma_start(bias[:, :], ln_bias[0].partition_broadcast(P)).then_inc(ln_in, 16)

            def load_residual(i):
                if i >= 2:
                    sp.wait_ge(stored[i % 2], 16 * (i // 2))
                sp.dma_start(res[i % 2][:, :], x[0, i * P:(i + 1) * P, :]).then_inc(res_in[i % 2], 16)

            load_residual(0)
            load_residual(1)
            for i in range(NB):
                sp.wait_ge(finished, i + 1)
                sp.dma_start(out[0, i * P:(i + 1) * P, :], res[i % 2][:, :]).then_inc(stored[i % 2], 16)
                if i + 2 < NB:
                    load_residual(i + 2)
            for s in range(2):
                sp.wait_ge(stored[s], 16 * (NB // 2))

        @block.tensor
        def _(pe):
            def three_passes(dst, pairs):
                last = len(pairs) - 1
                for n, (s_hi, s_lo, m_hi, m_lo) in enumerate(pairs):
                    pe.matmul(dst, s_hi, m_hi, start=(n == 0), stop=False)
                    pe.matmul(dst, s_hi, m_lo, start=False, stop=False)
                    mm = pe.matmul(dst, s_lo, m_hi, start=False, stop=(n == last))
                return mm

            def transpose_rows(r):
                pe.wait_ge(rows_in[r % 2], 16 * (r // 2 + 1))
                for h in range(2):
                    n, bank = bank_of(narrow, plan.narrow, ("rows", r, h))
                    if n >= 2:
                        pe.wait_ge(narrow_read[n % 2], n // 2)
                    for j in range(4):
                        k = 4 * h + j
                        t = pe.transpose(bank[:, j * P:(j + 1) * P], rows[r % 2][:, k * P:(k + 1) * P], ident[:, :])
                    t.then_inc(narrow_full, 1)

            def project(n):
                c, i = jobs[n]
                of_mem, s = kinds[c][1], slot_of(c)
                split = plan.narrow["rows", (0 if of_mem else NBM) + i, 1]
                pe.wait_ge(narrow_read[split % 2], split // 2 + 1)
                _, bank = bank_of(wide, plan.wide, ("job", n))
                if n >= 3:
                    pe.wait_ge(h_read, n - 2)
                t_hi, t_lo = (mem_hi, mem_lo) if of_mem else (x_hi, x_lo)
                cols = slice(i * P, (i + 1) * P)
                for h in range(2):
                    pe.wait_ge(chunk_rounded, 2 * c + h + 1)
                    pe.wait_ge(chunk_split, 2 * c + h + 1)
                    for k in range(h * KT // 2, (h + 1) * KT // 2):
                        dst = bank[:, 0:C]
                        pe.matmul(dst, t_hi[:, k, cols], w_hi[s][:, k, :], start=(k == 0), stop=False)
                        pe.matmul(dst, t_hi[:, k, cols], w_lo[s][:, k, :], start=False, stop=False)
                        mm = pe.matmul(dst, t_lo[:, k, cols], w_hi[s][:, k, :], start=False, stop=(k == KT - 1))
                mm.then_inc(wide_full, 1)

            def transpose_keys(k):
                _, heads = key_dst(k)
                if k < NBM:
                    pe.wait_ge(h_read, plan.key_jobs[k] + 1)
                else:
                    pe.wait_ge(keys_rotated, k - NBM + 1)
                n, bank = bank_of(narrow, plan.narrow, ("keys", k))
                if n >= 2:
                    pe.wait_ge(narrow_read[n % 2], n // 2)
                for h in range(heads):
                    twice = keys2[k % 2][:, h, :, :].rearrange("p a d -> p (a d)")
                    t = pe.transpose(bank[:, h * P:(h + 1) * P], twice, ident[:, :])
                t.then_inc(narrow_full, 1)

            pe.wait_ge(ident_in, 16)
            for what, n in plan.steps:
                {"rows": transpose_rows, "job": project, "keys": transpose_keys}[what](n)

            for f in range(FT):
                pe.wait_ge(gate_rounded, f + 1)
                pe.wait_ge(gate_split, f + 1)
                for h in range(2):
                    n = 2 * f + h
                    _, bank = bank_of(wide, plan.wide, ("gate", n))
                    if n < 3:
                        pe.wait_ge(h_read, n_jobs + n - 2)
                    else:
                        pe.wait_ge(gate_done, n - 2)
                    cols = slice(h * HALF, (h + 1) * HALF)
                    three_passes(bank[:, :], [(g_hi[f % 2][:, k, :], g_lo[f % 2][:, k, :], x_hi[:, k, cols],
                                               x_lo[:, k, cols]) for k in range(KT)])\
                        .then_inc(wide_full, 1)

            def transpose_q(u):
                heads = UNITS[u][3]
                n, bank = bank_of(narrow, plan.narrow, ("q", u))
                if n >= 2:
                    pe.wait_ge(narrow_read[n % 2], n // 2)
                pe.wait_ge(q_twice, u + 1)
                for hh in range(heads):
                    twice = q2[u % 2][:, hh, :, :].rearrange("p a d -> p (a d)")
                    t = pe.transpose(bank[:, hh * P:(hh + 1) * P], twice, ident[:, :])
                t.then_inc(narrow_full, 1)

            def score(u):
                kind, i, h0, heads, nk = UNITS[u]
                split = plan.narrow["q", u]
                pe.wait_ge(narrow_read[split % 2], split // 2 + 1)
                if u >= 2:
                    pe.wait_ge(probs_ready, u - 1)
                for c, (lo, hi) in enumerate(key_chunks(u)):
                    n, bank = bank_of(wide, plan.wide, ("scores", u, c))
                    since = n - plan.wide["scores", 0, 0]
                    if since < 3:
                        pe.wait_ge(gate_done, 2 * FT + since - 2)
                    for hh in range(heads):
                        h = h0 + hh
                        if kind == "a":
                            dst = bank[:, hh * C:hh * C + nk * P]
                            keys = k_a[:, h // (HA // GA), (i + 1 - nk) * P:(i + 1) * P]
                        elif kind == "b":
                            dst, keys = bank[:, 0:hi - lo], k_b[:, h, lo:hi]
                        else:
                            dst, keys = bank[:, hh * C:(hh + 1) * C], k_c[:, h, :]
                        pe.matmul(dst, q_hi[u % 2][:, hh * P:(hh + 1) * P], keys, start=True, stop=False)
                        mm = pe.matmul(dst, q_lo[u % 2][:, hh * P:(hh + 1) * P], keys, start=False, stop=True)
                    mm.then_inc(wide_full, 1)

            def transpose_probs(u):
                pe.wait_ge(probs_ready, u + 1)
                tiles = prob_tiles(u)
                for c, _ in plan.pt_chunks(u):
                    n, bank = bank_of(narrow, plan.narrow, ("probs", u, c))
                    if n >= 2:
                        pe.wait_ge(narrow_read[n % 2], n // 2)
                    for j, (_, _, col) in enumerate(tiles[4 * c:4 * c + 4]):
                        t = pe.transpose(bank[:, j * P:(j + 1) * P], prob[u % 2][:, col:col + P], ident[:, :])
                    t.then_inc(narrow_full, 1)

            def times_v(u):
                heads = UNITS[u][3]
                for c, _ in plan.pt_chunks(u):
                    n = plan.narrow["probs", u, c]
                    pe.wait_ge(narrow_read[n % 2], n // 2 + 1)
                if u >= 2:
                    pe.wait_ge(o_done, u - 1)
                tiles = prob_tiles(u)
                for hh in range(heads):
                    mine = [(n, t) for n, (h, t, _) in enumerate(tiles) if h == hh]
                    for n, t in mine:
                        w = plan.pt[u, n // 4] % 4
                        mm = pe.matmul(o_ps[u % 2][:, hh * HD:(hh + 1) * HD],
                                       prob_t[w][:, (n % 4) * P:(n % 4 + 1) * P], v_tile(u, t, hh),
                                       start=(n == mine[0][0]), stop=(n == mine[-1][0]))
                mm.then_inc(pv_done, 1)

            def transpose_y(i):
                pe.wait_ge(o_scaled, i + 1)
                for h in range(2):
                    n, bank = bank_of(narrow, plan.narrow, ("y", i, h))
                    if n >= 2:
                        pe.wait_ge(narrow_read[n % 2], n // 2)
                    for j in range(4):
                        f = 4 * h + j
                        t = pe.transpose(bank[:, j * P:(j + 1) * P], qo[:, i, f * P:(f + 1) * P], ident[:, :])
                    t.then_inc(narrow_full, 1)

            def project_out(i, piece):
                half, p = divmod(piece, PIECES // 2)
                passes = [(y_hi[:, i, k, :], wo_hi, k) for k in range(FT)] + \
                         [(y_hi[:, i, k, :], wo_lo, k) for k in range(FT)] + \
                         [(y_lo[:, k, i * P:(i + 1) * P], wo_hi, k) for k in range(FT)]
                if p == 0:
                    pe.wait_ge(y_split, i + 1)
                    pe.wait_ge(wo_split, FT)
                    if 2 * i + half:
                        pe.wait_ge(res_sum, 2 * i + half)
                size = -(-len(passes) // (PIECES // 2))
                for n in range(p * size, min((p + 1) * size, len(passes))):
                    y, w, k = passes[n]
                    mm = pe.matmul(out_ps[:, :], y, w[:, k, half * HALF:(half + 1) * HALF],
                                   start=(n == 0), stop=(n == len(passes) - 1))
                if p == PIECES // 2 - 1:
                    mm.then_inc(out_full, 1)

            pe.wait_ge(h_read, n_jobs)
            last = plan.narrow["keys", len(plan.key_jobs) - 1]
            pe.wait_ge(narrow_read[last % 2], last // 2 + 1)
            for v in range(ITERATIONS):
                if v < n_units:
                    transpose_q(v)
                if 0 <= v - 1 < n_units:
                    score(v - 1)
                if 0 <= v - 2 < n_units:
                    transpose_probs(v - 2)
                if 0 <= v - 3 < n_units:
                    times_v(v - 3)
                if block_at(v, AT_Y) is not None:
                    transpose_y(block_at(v, AT_Y))
                for p in range(PIECES):
                    if block_at(v, AT_OUT + p) is not None:
                        project_out(block_at(v, AT_OUT + p), p)

        @block.scalar
        def _(act):
            nc.scalar.preload_act_table_set("natural_log_exp_and_others")

            def chunk_hi(c):
                s = slot_of(c)
                for h in range(2):
                    act.wait_ge(chunk_in[s][h], 16 * (c // 3 + 1))
                    k = slice(h * KT // 2, (h + 1) * KT // 2)
                    act.activation(w_hi[s][:, k, :], w_raw[s][:, k, :], ACT.Copy).then_inc(chunk_rounded, 1)

            def rows_hi(r):
                for h in range(2):
                    act.wait_ge(narrow_full, plan.narrow["rows", r, h] + 1)
                    _, bank = bank_of(narrow, plan.narrow, ("rows", r, h))
                    dst, i = (mem_hi, r) if r < NBM else (x_hi, r - NBM)
                    act.activation(dst[:, 4 * h:4 * h + 4, i * P:(i + 1) * P],
                                   bank[:, :].rearrange("p (k t) -> p k t", k=4), ACT.Copy)\
                       .then_inc(rows_rounded, 1)

            def keys_hi(k):
                dst, heads = key_dst(k)
                act.wait_ge(narrow_full, plan.narrow["keys", k] + 1)
                _, bank = bank_of(narrow, plan.narrow, ("keys", k))
                act.activation(dst, bank[:, 0:heads * P].rearrange("p (h t) -> p h t", h=heads), ACT.Copy)\
                   .then_inc(keys_rounded, 1)

            def gate_hi(f):
                act.wait_ge(gate_in[f % 2], 16 * (f // 2 + 1))
                act.activation(g_hi[f % 2][:, :, :], g_raw[f % 2][:, :, :], ACT.Copy).then_inc(gate_rounded, 1)

            split_at = {0: -1, 1: 0, 2: 1}
            for c in range(3, len(kinds)):
                split_at[c] = plan.last_job[c - 1] - 4
            chunk_hi(0)
            for what, n in plan.steps:
                if what == "rows":
                    rows_hi(n)
                elif what == "keys":
                    keys_hi(n)
                else:
                    for c, job in split_at.items():
                        if job == n:
                            chunk_hi(c)
                    if n == n_jobs - 4:
                        gate_hi(0)
                    if n == n_jobs - 3:
                        gate_hi(1)

            act.wait_ge(negated, 2)
            for f in range(FT):
                for h in range(2):
                    n = 2 * f + h
                    act.wait_ge(wide_full, plan.wide["gate", n] + 1)
                    _, bank = bank_of(wide, plan.wide, ("gate", n))
                    if n >= 2:
                        act.wait_ge(gate_done, n - 1)
                    act.activation(gate_e[n % 2][:, :], bank[:, :], ACT.Exp, bias=neg_z_bias[:, f:f + 1], scale=-1.0)\
                       .then_inc(gate_exp, 1)
                if f + 2 < FT:
                    gate_hi(f + 2)

            def unit_q_hi(u):
                heads = UNITS[u][3]
                act.wait_ge(narrow_full, plan.narrow["q", u] + 1)
                _, bank = bank_of(narrow, plan.narrow, ("q", u))
                if u >= 2:
                    act.wait_ge(wide_full, scores_turn(u - 2) + 1)
                act.activation(q_hi[u % 2][:, 0:heads * P], bank[:, 0:heads * P], ACT.Copy, scale=SCALE)\
                   .then_inc(q_rounded, 1)

            def unit_exp(u):
                kind, _, _, heads, nk = UNITS[u]
                s, r = u % 2, u % 4
                act.wait_ge(neg_max, u + 1)
                if kind == "c":
                    _, bank = bank_of(wide, plan.wide, ("scores", u, 0))
                    if u >= 2:
                        act.wait_ge(narrow_full, probs_turn(u - 2) + 1)
                if u >= 4:
                    act.wait_ge(o_done, u - 3)
                for hh in range(heads):
                    cols = slice(hh * C, hh * C + nk * P)
                    src = bank[:, cols] if kind == "c" else prob[s][:, cols]
                    e = act.activation(prob[s][:, cols], src, ACT.Exp, bias=nb[:, r, hh:hh + 1],
                                       accum_out=den[:, r, hh:hh + 1])
                e.then_inc(probs_ready, 1)
                if kind == "a":
                    act.wait_ge(sink_gap_ready, a_index[u] + 1)
                    act.activation(gap_exp[:, r, :], gap[:, r, :], ACT.Exp).then_inc(sink_exp_ready, 1)

            def unit_pt(u):
                for c, w in plan.pt_chunks(u):
                    if w % 2 == 0:
                        act.wait_ge(narrow_full, plan.narrow["probs", u, c] + 1)
                        n, bank = bank_of(narrow, plan.narrow, ("probs", u, c))
                        if w >= 4:
                            act.wait_ge(pv_done, plan.pt_unit[w - 4] + 1)
                        size = P * len(prob_tiles(u)[4 * c:4 * c + 4])
                        act.activation(prob_t[w % 4][:, 0:size], bank[:, 0:size], ACT.Copy).then_inc(narrow_read[n % 2], 1)

            def block_rms(i):
                act.wait_ge(o_done, UB * (i + 1))
                for j, (lo, n) in enumerate(((0, W_A), (W_A, W_B), (W_A + W_B, W_C))):
                    sqr = act.activation(square_out[:, lo:lo + n], qo[:, i, lo:lo + n], ACT.Square, scale=float(n) ** -0.5,
                                         accum_out=sq[:, i % 2, j:j + 1])
                sqr.then_inc(squares, 1)
                act.wait_ge(squares, i + 1)
                act.activation(rms_log[:, i % 2, :], sq[:, i % 2, :], ACT.Ln, bias=RMS_EPS).then_inc(rms_logged, 1)
                act.wait_ge(rms_logged, i + 1)
                act.activation(rms[:, i % 2, :], rms_log[:, i % 2, :], ACT.Exp, scale=-0.5).then_inc(rms_ready, 1)

            for v in range(ITERATIONS):
                if v < n_units:
                    unit_q_hi(v)
                if 0 <= v - 1 < n_units:
                    unit_exp(v - 1)
                if 0 <= v - 2 < n_units:
                    unit_pt(v - 2)
                if 0 <= v - WO_FIRST < FT:
                    k = v - WO_FIRST
                    if k == 0:
                        act.wait_ge(wo_in, 16)
                        act.wait_ge(gate_cols_in, 32)
                    act.activation(wo_hi[:, k, :], wo_raw[:, k, :], ACT.Copy, scale=g_col[:, k:k + 1])\
                       .then_inc(wo_rounded, 1)
                i = block_at(v, AT_RMS)
                if i is not None:
                    block_rms(i)
                i = block_at(v, AT_YSPLIT)
                if i is not None:
                    n = plan.narrow["y", i, 1]
                    act.wait_ge(narrow_read[n % 2], n // 2 + 1)
                    act.activation(y_hi[:, i, :, :], zt[:, :, i * P:(i + 1) * P], ACT.Copy).then_inc(y_rounded, 1)
                i = block_at(v, AT_STATS)
                if i is not None:
                    s = i % 2
                    act.wait_ge(ln_stats, i + 1)
                    act.activation(ln_log[:, s:s + 1], moments[:, s, 1:2], ACT.Ln, bias=LN_EPS).then_inc(ln_logged, 1)
                    act.wait_ge(ln_logged, i + 1)
                    act.activation(ln_rstd[:, s:s + 1], ln_log[:, s:s + 1], ACT.Exp, scale=-0.5)\
                       .then_inc(ln_rstd_ready, 1)
                i = block_at(v, AT_NORM)
                if i is not None:
                    s = i % 2
                    act.wait_ge(ln_shift_ready, i + 1)
                    act.activation(res[s][:, :], res[s][:, :], ACT.Identity, bias=ln_shift[:, s:s + 1],
                                   scale=ln_rstd[:, s:s + 1]).then_inc(normed, 1)

        @block.vector
        def _(dve):
            def rows_lo(r):
                for h in range(2):
                    dve.wait_ge(rows_rounded, 2 * r + h + 1)
                    n, bank = bank_of(narrow, plan.narrow, ("rows", r, h))
                    hi, lo, i = (mem_hi, mem_lo, r) if r < NBM else (x_hi, x_lo, r - NBM)
                    ks, cols = slice(4 * h, 4 * h + 4), slice(i * P, (i + 1) * P)
                    dve.tensor_tensor(lo[:, ks, cols], bank[:, :].rearrange("p (k t) -> p k t", k=4),
                                      f32(hi[:, ks, cols]), ALU.subtract).then_inc(narrow_read[n % 2], 1)

            def keys_lo(k):
                dst, heads = key_dst(k)
                dve.wait_ge(keys_rounded, k + 1)
                n, bank = bank_of(narrow, plan.narrow, ("keys", k))
                dve.tensor_tensor(dst[HD:P], bank[HD:P, 0:heads * P].rearrange("p (h t) -> p h t", h=heads),
                                  f32(dst[HD:P]), ALU.subtract).then_inc(narrow_read[n % 2], 1)

            rotations = [0]

            def finish_job(n):
                c, i = jobs[n]
                kind, of_mem, col, q_col = kinds[c]
                dve.wait_ge(wide_full, plan.wide["job", n] + 1)
                _, bank = bank_of(wide, plan.wide, ("job", n))
                if n == NBM * 2:
                    dve.wait_ge(bias_in, 16)
                    dve.wait_ge(rope_in, 16)
                k = plan.key_jobs.index(n) if n in plan.key_jobs else None
                if k is not None and k >= 2:
                    dve.wait_ge(narrow_full, plan.narrow["keys", k - 2] + 1)
                if kind == "mk":
                    dve.tensor_copy(keys2[k % 2][:, :, :, :],
                                    heads_view(bank[:, 0:C], HC).unsqueeze(2).to_broadcast([P, HC, 2, HD]))\
                       .then_inc(h_read, 1)
                elif kind == "mv":
                    dve.tensor_copy(v_c[:, i, :], bank[:, 0:C]).then_inc(h_read, 1)
                else:
                    b = b_row[:, col:col + C]
                    dst = {"vb": v_b[:, i, :], "qc": qo[:, i, q_col:q_col + C] if q_col is not None else None}\
                        .get(kind, h_sb[:, :])
                    if kind == "kva":
                        dve.tensor_tensor(v_a[:, i, :], bank[:, W_KV:C], b[:, W_KV:C], ALU.add)
                        dst, b = h_sb[:, 0:W_KV], b[:, 0:W_KV]
                    dve.tensor_tensor(dst, bank[:, 0:b.shape[1]], b, ALU.add).then_inc(h_read, 1)
                if kind in ("kva", "kb", "q"):
                    m = rotations[0]
                    rotations[0] += 1
                    width = W_KV if kind == "kva" else C
                    nh = width // HD
                    dve.wait_ge(h_read, n + 1)
                    h3 = heads_view(h_sb[:, 0:width], nh)
                    r3, s3 = heads_view(rot_cos[:, 0:width], nh), heads_view(rot_sin[:, 0:width], nh)
                    tab = rope[:, i, :]

                    def per_head(lo, hi):
                        return tab[:, lo:hi].unsqueeze(1).to_broadcast([P, nh, hi - lo])

                    half = HD // 2
                    dve.tensor_tensor(r3, h3, per_head(0, HD), ALU.mult)
                    dve.tensor_tensor(s3[:, :, 0:half], h3[:, :, half:HD], per_head(HD, HD + half), ALU.mult)
                    dve.tensor_tensor(s3[:, :, half:HD], h3[:, :, 0:half], per_head(HD + half, 2 * HD), ALU.mult)\
                       .then_inc(rope_parts, 1)
                    dve.wait_ge(rope_parts, m + 1)
                    if k is not None:
                        shape = [P, nh, 2, HD]
                        dve.tensor_tensor(keys2[k % 2][:, 0:nh, :, :], r3.unsqueeze(2).to_broadcast(shape),
                                          s3.unsqueeze(2).to_broadcast(shape), ALU.add).then_inc(keys_rotated, 1)
                    else:
                        dve.tensor_tensor(qo[:, i, q_col:q_col + C], rot_cos[:, :], rot_sin[:, :], ALU.add)\
                           .then_inc(q_rotated, 1)

            for what, n in plan.steps:
                {"rows": rows_lo, "job": finish_job, "keys": keys_lo}[what](n)

            dve.wait_ge(gate_cols_in, 32)
            dve.wait_ge(sinks_in, 16)
            dve.tensor_scalar(neg_z_bias[:, :], z_bias[:, :], -1.0, None, ALU.mult).then_inc(negated, 1)
            dve.tensor_scalar(neg_sink[:, :], sink_row[:, :], -1.0, None, ALU.mult).then_inc(negated, 1)
            for n in range(2 * FT):
                f, h = divmod(n, 2)
                _, bank = bank_of(wide, plan.wide, ("gate", n))
                e = gate_e[n % 2]
                dve.wait_ge(gate_exp, n + 1)
                dve.tensor_scalar(e[:, :], e[:, :], 1.0, None, ALU.add).then_inc(gate_plus_one, 1)
                dve.wait_ge(gate_plus_one, n + 1)
                dve.reciprocal(e[:, :], e[:, :]).then_inc(gate_inverted, 1)
                dve.wait_ge(gate_inverted, n + 1)
                dve.scalar_tensor_tensor(zt[:, f, h * HALF:(h + 1) * HALF], bank[:, :], z_bias[:, f:f + 1], e[:, :],
                                         ALU.add, ALU.mult).then_inc(gate_done, 1)

            def unit_q_lo(u):
                heads = UNITS[u][3]
                dve.wait_ge(q_rounded, u + 1)
                n, bank = bank_of(narrow, plan.narrow, ("q", u))
                if u >= 2:
                    dve.wait_ge(wide_full, scores_turn(u - 2) + 1)
                dve.scalar_tensor_tensor(q_lo[u % 2][:, 0:heads * P], bank[:, 0:heads * P], SCALE,
                                         f32(q_hi[u % 2][:, 0:heads * P]), ALU.mult, ALU.subtract)\
                   .then_inc(narrow_read[n % 2], 1)

            def unit_max(u):
                kind, i, h0, heads, nk = UNITS[u]
                s, r = u % 2, u % 4
                if u >= 4:
                    dve.wait_ge(probs_ready, u - 3)
                if kind == "c":
                    dve.wait_ge(wide_full, plan.wide["scores", u, 0] + 1)
                    _, bank = bank_of(wide, plan.wide, ("scores", u, 0))
                    dve.tensor_reduce(nb[:, r, :], heads_view(bank[:, 0:2 * C], 2), AX.X, ALU.max, negate=True)\
                       .then_inc(neg_max, 1)
                    return
                if u >= 2:
                    dve.wait_ge(narrow_full, probs_turn(u - 2) + 1)
                for c, (lo, hi) in enumerate(key_chunks(u)):
                    dve.wait_ge(wide_full, plan.wide["scores", u, c] + 1)
                    _, bank = bank_of(wide, plan.wide, ("scores", u, c))
                    if kind == "b":
                        off = (NB - nk) * P
                        ttr = dve.tensor_tensor_reduce(prob[s][:, lo:hi], bank[:, 0:hi - lo],
                                                       mask_b[:, off + lo:off + hi], 1.0, -3e38, ALU.add, ALU.max,
                                                       mx[:, s, c:c + 1])
                    else:
                        for hh in range(heads):
                            cols = slice(hh * C, hh * C + nk * P)
                            ttr = dve.tensor_tensor_reduce(prob[s][:, cols], bank[:, cols],
                                                           mask_a[:, (2 - nk) * P:2 * P], 1.0, -3e38, ALU.add,
                                                           ALU.max, mx[:, s, hh:hh + 1])
                ttr.then_inc(row_max, 1)
                dve.wait_ge(row_max, masked_index[u] + 1)
                if kind == "b":
                    dve.tensor_reduce(nb[:, r, 0:1], mx[:, s, 0:len(key_chunks(u))], AX.X, ALU.max, negate=True)\
                       .then_inc(neg_max, 1)
                else:
                    ns = neg_sink[:, h0:h0 + 2]
                    dve.scalar_tensor_tensor(nb[:, r, :], mx[:, s, :], -1.0, ns, ALU.mult, ALU.min)\
                       .then_inc(neg_max, 1)
                    dve.wait_ge(neg_max, u + 1)
                    dve.tensor_tensor(gap[:, r, :], nb[:, r, :], ns, ALU.subtract).then_inc(sink_gap_ready, 1)

            def unit_pt(u):
                for c, w in plan.pt_chunks(u):
                    if w % 2 == 1:
                        dve.wait_ge(narrow_full, plan.narrow["probs", u, c] + 1)
                        n, bank = bank_of(narrow, plan.narrow, ("probs", u, c))
                        if w >= 4:
                            dve.wait_ge(pv_done, plan.pt_unit[w - 4] + 1)
                        size = P * len(prob_tiles(u)[4 * c:4 * c + 4])
                        dve.tensor_copy(prob_t[w % 4][:, 0:size], bank[:, 0:size]).then_inc(narrow_read[n % 2], 1)

            def unit_out(u):
                kind, i, _, heads, _ = UNITS[u]
                r = u % 4
                dve.wait_ge(probs_ready, u + 1)
                total = den
                if kind == "a":
                    dve.wait_ge(sink_exp_ready, a_index[u] + 1)
                    dve.tensor_tensor(den_all[:, r, :], den[:, r, :], gap_exp[:, r, :], ALU.add)\
                       .then_inc(den_sum, 1)
                    dve.wait_ge(den_sum, a_index[u] + 1)
                    total = den_all
                dve.reciprocal(rden[:, r, 0:heads], total[:, r, 0:heads]).then_inc(den_rcp, 1)
                dve.wait_ge(den_rcp, u + 1)
                dve.wait_ge(pv_done, u + 1)
                col = q_cols(u, 0)
                dve.tensor_tensor(heads_view(qo[:, i, col:col + heads * HD], heads),
                                  heads_view(o_ps[u % 2][:, 0:heads * HD], heads),
                                  rden[:, r, 0:heads].unsqueeze(2).to_broadcast([P, heads, HD]), ALU.mult)\
                   .then_inc(o_done, 1)

            dve.wait_ge(negated, 2)
            dve.wait_ge(masks_in, 32)
            for v in range(ITERATIONS):
                for at_res, half in ((AT_RES0, 0), (AT_RES1, 1)):
                    i = block_at(v, at_res)
                    if i is not None:
                        cols = slice(half * HALF, (half + 1) * HALF)
                        dve.wait_ge(res_in[i % 2], 16 * (i // 2 + 1))
                        dve.wait_ge(out_full, 2 * i + half + 1)
                        dve.scalar_tensor_tensor(res[i % 2][:, cols], res[i % 2][:, cols], ALPHA, out_ps[:, :],
                                                 ALU.mult, ALU.add).then_inc(res_sum, 1)
                if v < n_units:
                    unit_q_lo(v)
                if 0 <= v - 1 < n_units:
                    unit_max(v - 1)
                if 0 <= v - 2 < n_units:
                    unit_pt(v - 2)
                if 0 <= v - 3 < n_units:
                    unit_out(v - 3)
                if 0 <= v - WO_FIRST < FT:
                    k = v - WO_FIRST
                    dve.wait_ge(wo_rounded, k + 1)
                    dve.scalar_tensor_tensor(wo_lo[:, k, :], wo_raw[:, k, :], g_col[:, k:k + 1], f32(wo_hi[:, k, :]),
                                             ALU.mult, ALU.subtract).then_inc(wo_split, 1)
                i = block_at(v, AT_SCALE)
                if i is not None:
                    dve.wait_ge(rms_ready, i + 1)
                    for j, (lo, n) in enumerate(((0, W_A), (W_A, W_B), (W_A + W_B, W_C))):
                        ts = dve.tensor_scalar(qo[:, i, lo:lo + n], qo[:, i, lo:lo + n], rms[:, i % 2, j:j + 1], None,
                                               ALU.mult)
                    ts.then_inc(o_scaled, 1)
                i = block_at(v, AT_Y)
                if i is not None:
                    for h in range(2):
                        dve.wait_ge(narrow_full, plan.narrow["y", i, h] + 1)
                        n, bank = bank_of(narrow, plan.narrow, ("y", i, h))
                        z = zt[:, 4 * h:4 * h + 4, i * P:(i + 1) * P]
                        dve.tensor_tensor(z, bank[:, :].rearrange("p (f t) -> p f t", f=4), z, ALU.mult)\
                           .then_inc(narrow_read[n % 2], 1)
                i = block_at(v, AT_STATS)
                if i is not None:
                    s = i % 2
                    dve.wait_ge(res_sum, 2 * i + 2)
                    for h in range(2):
                        bs = dve.bn_stats(stats[:, s, h, :], res[s][:, h * HALF:(h + 1) * HALF])
                    bs.then_inc(ln_part, 1)
                    dve.wait_ge(ln_part, i + 1)
                    dve.bn_aggr(moments[:, s, :], stats[:, s, :, :]).then_inc(ln_stats, 1)
                i = block_at(v, AT_NORM)
                if i is not None:
                    s = i % 2
                    dve.wait_ge(ln_rstd_ready, i + 1)
                    dve.scalar_tensor_tensor(ln_shift[:, s:s + 1], moments[:, s, 0:1], -1.0, ln_rstd[:, s:s + 1],
                                             ALU.mult, ALU.mult).then_inc(ln_shift_ready, 1)

        @block.gpsimd
        def _(pool):
            for c in range(len(kinds)):
                s = slot_of(c)
                for h in range(2):
                    pool.wait_ge(chunk_rounded, 2 * c + h + 1)
                    k = slice(h * KT // 2, (h + 1) * KT // 2)
                    pool.tensor_tensor(w_lo[s][:, k, :], w_raw[s][:, k, :], f32(w_hi[s][:, k, :]), ALU.subtract)\
                        .then_inc(chunk_split, 1)
            for f in range(FT):
                pool.wait_ge(gate_rounded, f + 1)
                pool.tensor_tensor(g_lo[f % 2][:, :, :], g_raw[f % 2][:, :, :], f32(g_hi[f % 2][:, :, :]),
                                   ALU.subtract).then_inc(gate_split, 1)

            def unit_q_twice(u):
                _, i, _, heads, _ = UNITS[u]
                if u >= 2:
                    pool.wait_ge(narrow_full, plan.narrow["q", u - 2] + 1)
                q = heads_view(qo[:, i, q_cols(u, 0):q_cols(u, 0) + heads * HD], heads)
                pool.tensor_copy(q2[u % 2][:, 0:heads, :, :], q.unsqueeze(2).to_broadcast([P, heads, 2, HD]))\
                    .then_inc(q_twice, 1)

            pool.wait_ge(q_rotated, 3 * NB)
            pool.wait_ge(h_read, n_jobs)
            unit_q_twice(0)
            for v in range(ITERATIONS):
                if v + 1 < n_units:
                    unit_q_twice(v + 1)
                i = block_at(v, AT_YSPLIT)
                if i is not None:
                    pool.wait_ge(y_rounded, i + 1)
                    cols = slice(i * P, (i + 1) * P)
                    pool.tensor_tensor(y_lo[:, :, cols], zt[:, :, cols], f32(y_hi[:, i, :, :]), ALU.subtract)\
                        .then_inc(y_split, 1)
                i = block_at(v, AT_NORM)
                if i is not None:
                    s = i % 2
                    if i == 0:
                        pool.wait_ge(ln_in, 32)
                    pool.wait_ge(normed, i + 1)
                    pool.tensor_tensor(res[s][:, :], res[s][:, :], gain[:, :], ALU.mult).then_inc(gained, 1)
                    pool.wait_ge(gained, i + 1)
                    pool.tensor_tensor(res[s][:, :], res[s][:, :], bias[:, :], ALU.add).then_inc(finished, 1)


def rope_table():
    pos = np.arange(SEQ, dtype=np.float32)
    inv = np.float32(10000.0) ** (-np.arange(0, HD, 2, dtype=np.float32) / np.float32(HD))
    ang = pos[:, None] * inv[None, :].astype(np.float32)
    c, s = np.cos(ang), np.sin(ang)
    return np.concatenate([c, c, -s, s], axis=1).astype(np.float32)


def masks():
    p = np.arange(P)[:, None]
    d = p + P - np.arange(2 * P)[None, :]
    a = np.where((d >= 0) & (d < WINDOW), 0.0, MASKED).astype(np.float32)
    d = p + (NB - 1) * P - np.arange(SEQ)[None, :]
    count = sum(((d >= 0) & (d <= w) & (d % r == 0)).astype(np.float64) for w, r in PAIRS)
    b = np.where(count > 0, np.log(np.maximum(count, 1.0)), MASKED).astype(np.float32)
    return a, b


_INS = ["x", "mem", "w_in", "b_in", "w_mem", "attn_sinks", "g_branch", "w_out", "ln_gain", "ln_bias"]


def kernel(**inputs):
    import concourse.bacc as bacc
    from concourse.bass_utils import run_bass_kernel_spmd

    nc = bacc.Bacc("TRN2", target_bir_lowering=False, num_devices=1, dynamic_dma_scratch_size=1024)
    mask_a, mask_b = masks()
    arrays = {name: np.ascontiguousarray(inputs[name]) for name in _INS}
    arrays |= {"ident": np.eye(P, dtype=np.float32), "rope": rope_table(), "mask_a": mask_a, "mask_b": mask_b}
    arrays = {f"in_{name}": a for name, a in arrays.items()}
    args = [nc.dram_tensor(name, a.shape, mybir.dt.from_np(a.dtype), kind="ExternalInput").ap()
            for name, a in arrays.items()]
    out = nc.dram_tensor("out", (1, SEQ, DM), F32, kind="ExternalOutput").ap()
    layer(nc, *args, out)
    r = run_bass_kernel_spmd(nc, [arrays], core_ids=[0])
    return r.results[0]["out"]
```

```python
from contextlib import ExitStack

import numpy as np

import concourse.bass as bass
from concourse import mybir

F32 = mybir.dt.float32
F32R = mybir.dt.float32r
ALU = mybir.AluOpType
ACT = mybir.ActivationFunctionType
AX = mybir.AxisListType

P = 128
SEQ = 1024
DM = 1024
MEM = 256
NB = SEQ // P
NBM = MEM // P
KT = DM // P
HD = 64
HA, GA = 8, 2
HB = 4
HC = 4
WINDOW = 128
PAIRS = ((128, 1), (512, 4), (2048, 16))
DEPTH = 1
ALPHA = float((2 * DEPTH) ** 0.25)
RMS_EPS = 1e-6
LN_EPS = 1e-5
SCALE = HD ** -0.5
MASKED = -1e30
C = 256
HALF = 512

W_A, W_KV, W_B, W_C = HA * HD, GA * HD, HB * HD, HC * HD
COL_QA, COL_KA, COL_VA = 0, W_A, W_A + W_KV
COL_QB = COL_VA + W_KV
COL_KB, COL_VB = COL_QB + W_B, COL_QB + 2 * W_B
COL_QC = COL_VB + W_B
COL_Z = COL_QC + W_C
QKV = COL_Z
FT = (W_A + W_B + W_C) // P


def chunks():
    return [("mk", True, 0, None), ("mv", True, W_C, None),
            ("kva", False, COL_KA, None), ("kb", False, COL_KB, None), ("vb", False, COL_VB, None),
            ("q", False, COL_QA, 0), ("q", False, COL_QA + C, C), ("q", False, COL_QB, W_A),
            ("qc", False, COL_QC, W_A + W_B)]


def units():
    out = []
    for i in range(NB):
        window = min(i + 1, 2)
        a = [("a", i, 2 * j, 2, window) for j in range(HA // 2)]
        b = [("b", i, j, 1, i + 1) for j in range(HB)]
        c = [("c", i, 2 * j, 2, NBM) for j in range(HC // 2)]
        out += [a[0], b[0], a[1], b[1], a[2], b[2], a[3], b[3], c[0], c[1]]
    return out


UNITS = units()
UB = len(UNITS) // NB
GATE_ITERATIONS = 2
QS = 3
Q2 = 4
GATES = 2 * FT
WO_FIRST = GATE_ITERATIONS * GATES + 2
WO_TILES = 2
OUT_ITERATIONS = [6] * (NB - 3) + [9, 6, 1]
OUT_AT = [WO_FIRST + FT // WO_TILES]
for block in range(1, NB):
    OUT_AT.append(max(OUT_AT[-1] + OUT_ITERATIONS[block - 1], UB * (block + 1) + 9))
RMS_AT = [v - 5 for v in OUT_AT]
SCALE_AT = [v - 4 for v in OUT_AT]
Y_AT = [v - 3 for v in OUT_AT]
YSPLIT_AT = [v - 2 for v in OUT_AT]
RES_AT = [[v + -(-n // 2) for v, n in zip(OUT_AT, OUT_ITERATIONS)],
          [v + n for v, n in zip(OUT_AT, OUT_ITERATIONS)]]
STATS_AT = RES_AT[1]
NORM_AT = [v + 1 for v in STATS_AT]
ITERATIONS = NORM_AT[-1] + 1


def block_at(v, stage_at):
    return stage_at.index(v) if v in stage_at else None


def wo_tiles(v):
    first = (v - WO_FIRST) * WO_TILES
    return list(range(first, first + WO_TILES)) if 0 <= first < FT else []


def key_chunks(u):
    kind, _, _, heads, nk = UNITS[u]
    if kind != "b":
        return [(0, C * (heads - 1) + nk * P)]
    return [(c, min(c + HALF, nk * P)) for c in range(0, nk * P, HALF)]


def prob_tiles(u):
    kind, i, _, heads, nk = UNITS[u]
    if kind == "b":
        return [(0, t, t * P) for t in range(nk)]
    first = i + 1 - nk if kind == "a" else 0
    return [(hh, first + t, hh * C + t * P) for hh in range(heads) for t in range(nk)]


class Plan:

    def __init__(self):
        self.chunks = chunks()
        self.jobs = [(c, i) for c, (_, of_mem, _, _) in enumerate(self.chunks)
                     for i in range(NBM if of_mem else NB)]
        self.last_job = {c: max(n for n, j in enumerate(self.jobs) if j[0] == c)
                         for c in range(len(self.chunks))}
        self.key_jobs = [n for n, (c, _) in enumerate(self.jobs)
                         if self.chunks[c][0] in ("mk", "kva", "kb")]
        self.steps = [("rows", 0), ("rows", 1), ("rows", 2)]
        for n in range(len(self.jobs)):
            if n and n + 2 < NBM + NB:
                self.steps.append(("rows", n + 2))
            self.steps.append(("job", n))
            if n - 1 in self.key_jobs:
                self.steps.append(("keys", self.key_jobs.index(n - 1)))
        wide, narrow = [], []
        for what, n in self.steps:
            if what == "rows":
                narrow += [("rows", n, h) for h in range(2)]
            else:
                (narrow if what == "keys" else wide).append((what, n))
        self.pt_unit = []
        self.pt = {}
        narrow.append(("q", 0))
        for v in range(ITERATIONS):
            if 0 <= v - 1 < len(UNITS):
                wide += [("scores", v - 1, c) for c in range(len(key_chunks(v - 1)))]
            if 0 <= v - 2 < len(UNITS):
                for c in range(-(-len(prob_tiles(v - 2)) // 4)):
                    self.pt[v - 2, c] = len(self.pt_unit)
                    self.pt_unit.append(v - 2)
                    narrow.append(("probs", v - 2, c))
            if v + 1 < len(UNITS):
                narrow.append(("q", v + 1))
            if block_at(v, Y_AT) is not None:
                narrow += [("y", block_at(v, Y_AT), h) for h in range(2)]
        self.wide = {key: n for n, key in enumerate(wide)}
        self.narrow = {key: n for n, key in enumerate(narrow)}
        for n, key in enumerate(wide):
            assert key[0] != "scores" or wide[n - 3][0] == "job" or wide[n - 3][1] <= key[1] - 2

    def pt_chunks(self, u):
        return [(c, self.pt[u, c]) for c in range(-(-len(prob_tiles(u)) // 4))]


def layer(nc, x, mem, w_in, b_in, w_mem, sinks, g_branch, w_out, ln_gain, ln_bias,
          ident_d, rope_d, mask_a_d, mask_b_d, out):
    plan = Plan()
    jobs, kinds = plan.jobs, plan.chunks
    n_jobs, n_units = len(jobs), len(UNITS)

    with ExitStack() as ctx:
        def sem(name):
            return ctx.enter_context(nc.semaphore(name))

        ident_in, bias_in, rope_in = sem("ident_in"), sem("bias_in"), sem("rope_in")
        gate_cols_in, sinks_in, masks_in = sem("gate_cols_in"), sem("sinks_in"), sem("masks_in")
        wo_in, ln_in = [sem(f"wo_in{k}") for k in range(FT)], sem("ln_in")
        rows_in = [sem(f"rows_in{s}") for s in range(2)]
        chunk_in = [[sem(f"chunk_in{s}{h}") for h in range(2)] for s in range(3)]
        gate_in = [sem(f"gate_in{s}") for s in range(2)]
        res_in = [sem(f"res_in{s}") for s in range(2)]
        stored = [sem(f"stored{s}") for s in range(2)]
        wide_full, narrow_full = sem("wide_full"), sem("narrow_full")
        gate_full, out_full = sem("gate_full"), sem("out_full")
        narrow_read = [sem(f"narrow_read{b}") for b in range(2)]
        rows_rounded, chunk_rounded, chunk_split = sem("rows_rounded"), sem("chunk_rounded"), sem("chunk_split")
        gate_rounded, gate_split, h_read = sem("gate_rounded"), sem("gate_split"), sem("h_read")
        rope_parts, keys_rotated, q_rotated = sem("rope_parts"), sem("keys_rotated"), sem("q_rotated")
        keys_rounded, negated, gate_exp = sem("keys_rounded"), sem("negated"), sem("gate_exp")
        gate_logged, gate_sigmoid, gate_done = sem("gate_logged"), sem("gate_sigmoid"), sem("gate_done")
        q_twice, q_rounded, row_max = sem("q_twice"), sem("q_rounded"), sem("row_max")
        neg_max, sink_gap_ready, sink_exp_ready = sem("neg_max"), sem("sink_gap_ready"), sem("sink_exp_ready")
        probs_ready, pv_done, den_sum = sem("probs_ready"), sem("pv_done"), sem("den_sum")
        den_rcp, o_done = sem("den_rcp"), sem("o_done")
        squares, rms_logged, rms_ready = sem("squares"), sem("rms_logged"), sem("rms_ready")
        o_scaled, y_rounded, y_split = sem("o_scaled"), sem("y_rounded"), sem("y_split")
        wo_rounded, wo_split = sem("wo_rounded"), sem("wo_split")
        res_sum, ln_part, ln_stats = sem("res_sum"), sem("ln_part"), sem("ln_stats")
        ln_logged, ln_rstd_ready, ln_shift_ready = sem("ln_logged"), sem("ln_rstd_ready"), sem("ln_shift_ready")
        normed, gained, finished = sem("normed"), sem("gained"), sem("finished")

        top = -(-nc.sbuf_base // 32) * 32

        def at(name, shape, dt, offset):
            return nc.alloc_sbuf_tensor_at(name, shape, dt, offset=offset)

        class Region:
            def __init__(self, size):
                nonlocal top
                self.base, top = top, top + size
                self.end = top

        def nbytes(*shape):
            return 4 * int(np.prod(shape))

        r_x = Region(2 * nbytes(KT, SEQ))
        lo_half = r_x.base + nbytes(KT, SEQ)
        x_hi = at("x_hi", [P, KT, SEQ], F32R, r_x.base)
        x_lo = at("x_lo", [P, KT, SEQ], F32R, lo_half)
        wo_hi = at("wo_hi", [P, FT, DM], F32R, r_x.base)
        wo_raw = at("wo_raw", [P, FT, DM], F32, lo_half)
        wo_lo = at("wo_lo", [P, FT, DM], F32R, lo_half)
        r_q = Region(nbytes(NB, DM))
        qo = at("qo", [P, NB, DM], F32, r_q.base)
        y_hi = at("y_hi", [P, NB, FT, P], F32R, r_q.base)
        rows = [at(f"rows{s}", [P, DM], F32, r_q.base + s * nbytes(DM)) for s in range(2)]
        mem_hi = at("mem_hi", [P, KT, MEM], F32R, r_q.base + nbytes(4, DM))
        mem_lo = at("mem_lo", [P, KT, MEM], F32R, r_q.base + nbytes(6, DM))
        k_a = at("k_a", [P, GA, SEQ], F32R, Region(nbytes(GA, SEQ)).base)
        k_b = at("k_b", [P, HB, SEQ], F32R, Region(nbytes(HB, SEQ)).base)
        k_c = at("k_c", [P, HC, MEM], F32R, Region(nbytes(HC, MEM)).base)
        v_a = at("v_a", [P, NB, W_KV], F32, Region(nbytes(NB, W_KV)).base)
        v_b = at("v_b", [P, NB, W_B], F32, Region(nbytes(NB, W_B)).base)
        v_c = at("v_c", [P, NBM, W_C], F32, Region(nbytes(NBM, W_C)).base)
        r_z = Region(nbytes(FT, SEQ))
        zt = at("zt", [P, FT, SEQ], F32, r_z.base)
        y_lo = at("y_lo", [P, FT, SEQ], F32R, r_z.base)
        r_s = Region(4 * nbytes(DM))
        slot = [r_z.base, r_z.base + 2 * nbytes(KT, C), r_s.base]
        w_hi = [at(f"w_hi{s}", [P, KT, C], F32R, o) for s, o in enumerate(slot)]
        w_raw = [at(f"w_raw{s}", [P, KT, C], F32, o + nbytes(KT, C)) for s, o in enumerate(slot)]
        w_lo = [at(f"w_lo{s}", [P, KT, C], F32R, o + nbytes(KT, C)) for s, o in enumerate(slot)]
        gate = [r_s.base + s * 2 * nbytes(KT, P) for s in range(2)]
        g_hi = [at(f"g_hi{s}", [P, KT, P], F32R, o) for s, o in enumerate(gate)]
        g_raw = [at(f"g_raw{s}", [P, KT, P], F32, o + nbytes(KT, P)) for s, o in enumerate(gate)]
        g_lo = [at(f"g_lo{s}", [P, KT, P], F32R, o + nbytes(KT, P)) for s, o in enumerate(gate)]
        gain = at("gain", [P, DM], F32, r_s.base)
        bias = at("bias", [P, DM], F32, r_s.base + nbytes(DM))
        res = [at(f"res{s}", [P, DM], F32, r_s.base + (2 + s) * nbytes(DM)) for s in range(2)]
        r_t = Region(max(nbytes(QKV + 7 * C), nbytes(2 * SEQ + (2 * QS + Q2) * 2 * P)))
        b_row = at("b_row", [P, QKV], F32, r_t.base)
        h_at = r_t.base + nbytes(QKV)
        h_sb = at("h_sb", [P, C], F32, h_at)
        rot_cos = at("rot_cos", [P, C], F32, h_at + nbytes(C))
        rot_sin = at("rot_sin", [P, C], F32, h_at + 2 * nbytes(C))
        keys2 = [at(f"keys2{s}", [P, C // HD, 2, HD], F32, h_at + (3 + 2 * s) * nbytes(C)) for s in range(2)]
        prob = [at(f"prob{s}", [P, SEQ], F32, r_t.base + s * nbytes(SEQ)) for s in range(2)]
        q_at = r_t.base + 2 * nbytes(SEQ)
        q_hi = [at(f"q_hi{s}", [P, 2 * P], F32R, q_at + s * nbytes(2 * P)) for s in range(QS)]
        q_lo = [at(f"q_lo{s}", [P, 2 * P], F32R, q_at + (QS + s) * nbytes(2 * P)) for s in range(QS)]
        r_r = Region(nbytes(NB, 2 * HD))
        q2_at = q_at + 2 * QS * nbytes(2 * P)
        q2 = [at(f"q2{s}", [P, 2, 2, HD], F32, q2_at + s * nbytes(2 * P)) for s in range(Q2)]
        rope = at("rope", [P, NB, 2 * HD], F32, r_r.base)
        e_at = [Region(nbytes(HALF)).base for s in range(2)]
        gate_e = [at(f"gate_e{s}", [P, HALF], F32, e_at[s]) for s in range(2)]
        pt_at = [r_r.base, r_r.base + nbytes(HALF), Region(nbytes(HALF)).base, Region(nbytes(HALF)).base]
        prob_t = [at(f"prob_t{s}", [P, HALF], F32, o) for s, o in enumerate(pt_at)]
        mask_a = at("mask_a", [P, 2 * P], F32, Region(nbytes(2 * P)).base)
        mask_b = at("mask_b", [P, SEQ], F32, Region(nbytes(SEQ)).base)
        ident = at("ident", [P, P], F32, Region(nbytes(P)).base)

        def small(name, *shape):
            return at(name, [P, *shape], F32, Region(-(-nbytes(*shape) // 32) * 32).base)

        z_bias, neg_z_bias = small("z_bias", FT), small("neg_z_bias", FT)
        g_col = small("g_col", FT)
        sink_row, neg_sink = small("sink_row", HA), small("neg_sink", HA)
        mx = small("mx", 2, 2)
        nb = small("nb", 4, 2)
        gap, gap_exp = small("gap", 4, 2), small("gap_exp", 4, 2)
        den, den_all, rden = small("den", 4, 2), small("den_all", 4, 2), small("rden", 4, 2)
        sq = small("sq", 2, 3)
        rms_log, rms = small("rms_log", 2, 3), small("rms", 2, 3)
        square_out = at("square_out", [P, DM], mybir.dt.bfloat16, e_at[0])
        stats, moments = small("stats", 2, 2, 6), small("moments", 2, 2)
        ln_log, ln_rstd, ln_shift = small("ln_log", 2), small("ln_rstd", 2), small("ln_shift", 2)
        assert top <= nc.sbuf_usable_end, top

        wide = [ctx.enter_context(nc.psum_tensor(f"wide{b}", [P, HALF], F32)) for b in range(3)]
        narrow = [ctx.enter_context(nc.psum_tensor(f"narrow{b}", [P, HALF], F32)) for b in range(2)]
        long_ps = [ctx.enter_context(nc.psum_tensor(f"long_ps{b}", [P, HALF], F32)) for b in range(2)]
        o_ps = ctx.enter_context(nc.psum_tensor("o_ps", [P, HALF], F32))

        def f32(ap):
            return ap.bitcast(F32)

        def bank_of(ring, turns, key):
            n = turns[key]
            return n, ring[n % len(ring)]

        def slot_of(c):
            return (c + 2) % 3

        def heads_view(ap, n):
            return ap.rearrange("p (h d) -> p h d", h=n)

        def key_dst(k):
            c, i = jobs[plan.key_jobs[k]]
            t, n = {"mk": (k_c, HC), "kva": (k_a, GA), "kb": (k_b, HB)}[kinds[c][0]]
            return t[:, :, i * P:(i + 1) * P], n

        def v_tile(u, t, hh):
            kind, _, h0, _, _ = UNITS[u]
            h = h0 + hh
            if kind == "a":
                g = h // (HA // GA)
                return v_a[:, t, g * HD:(g + 1) * HD]
            return (v_b if kind == "b" else v_c)[:, t, h * HD:(h + 1) * HD]

        def q_cols(u, hh):
            kind, _, h0, _, _ = UNITS[u]
            return {"a": 0, "b": W_A, "c": W_A + W_B}[kind] + (h0 + hh) * HD

        a_index = {}
        masked_index = {}
        for u, unit in enumerate(UNITS):
            if unit[0] == "a":
                a_index[u] = len(a_index)
            if unit[0] != "c":
                masked_index[u] = len(masked_index)

        def scores_turn(u):
            return plan.wide["scores", u, len(key_chunks(u)) - 1]

        def probs_turn(u):
            return plan.narrow["probs", u, plan.pt_chunks(u)[-1][0]]

        block = ctx.enter_context(nc.Block())

        @block.sync
        def _(sp):
            def load_rows(r):
                if r >= 2:
                    sp.wait_ge(narrow_full, plan.narrow["rows", r - 2, 1] + 1)
                src = mem[0, r * P:(r + 1) * P, :] if r < NBM else \
                    x[0, (r - NBM) * P:(r - NBM + 1) * P, :]
                sp.dma_start(rows[r % 2][:, :], src).then_inc(rows_in[r % 2], 16)

            def load_chunk(c):
                if c >= 3:
                    sp.wait_ge(wide_full, plan.wide["job", plan.last_job[c - 3]] + 1)
                _, of_mem, col, _ = kinds[c]
                src = (w_mem if of_mem else w_in)[0, :, col:col + C]
                src = src.rearrange("(k p) n -> p k n", p=P)
                for h in range(2):
                    k = slice(h * KT // 2, (h + 1) * KT // 2)
                    sp.dma_start(w_raw[slot_of(c)][:, k, :], src[:, k, :])\
                      .then_inc(chunk_in[slot_of(c)][h], 16)

            def load_gate(f):
                if f < 2:
                    sp.wait_ge(wide_full, plan.wide["job", plan.last_job[6]] + 1)
                else:
                    sp.wait_ge(gate_full, 2 * (f - 2) + 2)
                src = w_in[0, :, COL_Z + f * P:COL_Z + (f + 1) * P]
                sp.dma_start(g_raw[f % 2][:, :, :], src.rearrange("(k p) n -> p k n", p=P))\
                  .then_inc(gate_in[f % 2], 16)

            load_rows(0)
            sp.dma_start(ident[:, :], ident_d).then_inc(ident_in, 16)
            load_chunk(0)
            load_rows(1)
            load_chunk(1)
            load_rows(2)
            load_chunk(2)
            load_rows(3)
            sp.dma_start(b_row[:, :], b_in[0, 0:QKV].partition_broadcast(P)).then_inc(bias_in, 16)
            load_rows(4)
            sp.dma_start(rope[:, :, :], rope_d.rearrange("(b p) d -> p b d", p=P)).then_inc(rope_in, 16)
            load_rows(5)
            load_rows(6)
            load_chunk(3)
            for r in range(7, NBM + NB):
                load_rows(r)
            with nc.allow_non_contiguous_dma(reason="one value per partition"):
                sp.dma_start(z_bias[:, :], b_in[0, COL_Z:].rearrange("(f p) -> p f", p=P))\
                  .then_inc(gate_cols_in, 16)
                sp.dma_start(g_col[:, :], g_branch[0].rearrange("(f p) -> p f", p=P))\
                  .then_inc(gate_cols_in, 16)
            sp.dma_start(sink_row[:, :], sinks[0].partition_broadcast(P)).then_inc(sinks_in, 16)
            sp.dma_start(mask_a[:, :], mask_a_d).then_inc(masks_in, 16)
            sp.dma_start(mask_b[:, :], mask_b_d).then_inc(masks_in, 16)
            for c in range(4, len(kinds)):
                load_chunk(c)
            for f in range(FT):
                load_gate(f)
            sp.wait_ge(gate_full, GATES)
            for k in range(FT):
                sp.dma_start(wo_raw[:, k, :], w_out[0, k * P:(k + 1) * P, :]).then_inc(wo_in[k], 16)
            sp.dma_start(gain[:, :], ln_gain[0].partition_broadcast(P)).then_inc(ln_in, 16)
            sp.dma_start(bias[:, :], ln_bias[0].partition_broadcast(P)).then_inc(ln_in, 16)

            def load_residual(i):
                if i >= 2:
                    sp.wait_ge(stored[i % 2], 16 * (i // 2))
                sp.dma_start(res[i % 2][:, :], x[0, i * P:(i + 1) * P, :]).then_inc(res_in[i % 2], 16)

            load_residual(0)
            load_residual(1)
            for i in range(NB):
                sp.wait_ge(finished, i + 1)
                sp.dma_start(out[0, i * P:(i + 1) * P, :], res[i % 2][:, :]).then_inc(stored[i % 2], 16)
                if i + 2 < NB:
                    load_residual(i + 2)
            for s in range(2):
                sp.wait_ge(stored[s], 16 * (NB // 2))

        @block.tensor
        def _(pe):
            def transpose_rows(r):
                pe.wait_ge(rows_in[r % 2], 16 * (r // 2 + 1))
                for h in range(2):
                    n, bank = bank_of(narrow, plan.narrow, ("rows", r, h))
                    if n >= 2:
                        pe.wait_ge(narrow_read[n % 2], n // 2)
                    for j in range(4):
                        k = 4 * h + j
                        t = pe.transpose(bank[:, j * P:(j + 1) * P], rows[r % 2][:, k * P:(k + 1) * P], ident[:, :])
                    t.then_inc(narrow_full, 1)

            def project(n):
                c, i = jobs[n]
                of_mem, s = kinds[c][1], slot_of(c)
                split = plan.narrow["rows", (0 if of_mem else NBM) + i, 1]
                pe.wait_ge(narrow_read[split % 2], split // 2 + 1)
                _, bank = bank_of(wide, plan.wide, ("job", n))
                if n >= 3:
                    pe.wait_ge(h_read, n - 2)
                t_hi, t_lo = (mem_hi, mem_lo) if of_mem else (x_hi, x_lo)
                cols = slice(i * P, (i + 1) * P)
                for h in range(2):
                    pe.wait_ge(chunk_rounded, 2 * c + h + 1)
                    pe.wait_ge(chunk_split, 2 * c + h + 1)
                    for k in range(h * KT // 2, (h + 1) * KT // 2):
                        dst = bank[:, 0:C]
                        pe.matmul(dst, t_hi[:, k, cols], w_hi[s][:, k, :], start=(k == 0), stop=False)
                        pe.matmul(dst, t_hi[:, k, cols], w_lo[s][:, k, :], start=False, stop=False)
                        mm = pe.matmul(dst, t_lo[:, k, cols], w_hi[s][:, k, :], start=False, stop=(k == KT - 1))
                mm.then_inc(wide_full, 1)

            def transpose_keys(k):
                _, heads = key_dst(k)
                if k < NBM:
                    pe.wait_ge(h_read, plan.key_jobs[k] + 1)
                else:
                    pe.wait_ge(keys_rotated, k - NBM + 1)
                n, bank = bank_of(narrow, plan.narrow, ("keys", k))
                if n >= 2:
                    pe.wait_ge(narrow_read[n % 2], n // 2)
                for h in range(heads):
                    twice = keys2[k % 2][:, h, :, :].rearrange("p a d -> p (a d)")
                    t = pe.transpose(bank[:, h * P:(h + 1) * P], twice, ident[:, :])
                t.then_inc(narrow_full, 1)

            pe.wait_ge(ident_in, 16)
            for what, n in plan.steps:
                {"rows": transpose_rows, "job": project, "keys": transpose_keys}[what](n)

            def gate_products(v, part):
                n, step = divmod(v, GATE_ITERATIONS)
                f, h = divmod(n, 2)
                shares = 2 * GATE_ITERATIONS
                share = 2 * step + part
                if share == 0:
                    pe.wait_ge(gate_rounded, f + 1)
                    pe.wait_ge(gate_split, f + 1)
                    if n >= 2:
                        pe.wait_ge(gate_done, n - 1)
                cols = slice(h * HALF, (h + 1) * HALF)
                dst = long_ps[n % 2][:, :]
                for k in range(share * KT // shares, (share + 1) * KT // shares):
                    pe.matmul(dst, g_hi[f % 2][:, k, :], x_hi[:, k, cols], start=(k == 0), stop=False)
                    pe.matmul(dst, g_hi[f % 2][:, k, :], x_lo[:, k, cols], start=False, stop=False)
                    mm = pe.matmul(dst, g_lo[f % 2][:, k, :], x_hi[:, k, cols], start=False, stop=(k == KT - 1))
                if share == shares - 1:
                    mm.then_inc(gate_full, 1)

            def transpose_q(u):
                heads = UNITS[u][3]
                n, bank = bank_of(narrow, plan.narrow, ("q", u))
                if n >= 2:
                    pe.wait_ge(narrow_read[n % 2], n // 2)
                pe.wait_ge(q_twice, u + 1)
                for hh in range(heads):
                    twice = q2[u % Q2][:, hh, :, :].rearrange("p a d -> p (a d)")
                    t = pe.transpose(bank[:, hh * P:(hh + 1) * P], twice, ident[:, :])
                t.then_inc(narrow_full, 1)

            def score(u):
                kind, i, h0, heads, nk = UNITS[u]
                split = plan.narrow["q", u]
                pe.wait_ge(narrow_read[split % 2], split // 2 + 1)
                if u == 0:
                    pe.wait_ge(h_read, n_jobs)
                    last = plan.narrow["keys", len(plan.key_jobs) - 1]
                    pe.wait_ge(narrow_read[last % 2], last // 2 + 1)
                if u >= 2:
                    pe.wait_ge(probs_ready, u - 1)
                for c, (lo, hi) in enumerate(key_chunks(u)):
                    _, bank = bank_of(wide, plan.wide, ("scores", u, c))
                    for hh in range(heads):
                        h = h0 + hh
                        if kind == "a":
                            dst = bank[:, hh * C:hh * C + nk * P]
                            keys = k_a[:, h // (HA // GA), (i + 1 - nk) * P:(i + 1) * P]
                        elif kind == "b":
                            dst, keys = bank[:, 0:hi - lo], k_b[:, h, lo:hi]
                        else:
                            dst, keys = bank[:, hh * C:(hh + 1) * C], k_c[:, h, :]
                        pe.matmul(dst, q_hi[u % QS][:, hh * P:(hh + 1) * P], keys, start=True, stop=False)
                        mm = pe.matmul(dst, q_lo[u % QS][:, hh * P:(hh + 1) * P], keys, start=False, stop=True)
                    mm.then_inc(wide_full, 1)

            def transpose_probs(u):
                pe.wait_ge(probs_ready, u + 1)
                tiles = prob_tiles(u)
                for c, _ in plan.pt_chunks(u):
                    n, bank = bank_of(narrow, plan.narrow, ("probs", u, c))
                    if n >= 2:
                        pe.wait_ge(narrow_read[n % 2], n // 2)
                    for j, (_, _, col) in enumerate(tiles[4 * c:4 * c + 4]):
                        t = pe.transpose(bank[:, j * P:(j + 1) * P], prob[u % 2][:, col:col + P], ident[:, :])
                    t.then_inc(narrow_full, 1)

            def times_v(u):
                heads = UNITS[u][3]
                for c, _ in plan.pt_chunks(u):
                    n = plan.narrow["probs", u, c]
                    pe.wait_ge(narrow_read[n % 2], n // 2 + 1)
                if u >= 1:
                    pe.wait_ge(o_done, u)
                tiles = prob_tiles(u)
                for hh in range(heads):
                    mine = [(n, t) for n, (h, t, _) in enumerate(tiles) if h == hh]
                    for n, t in mine:
                        w = plan.pt[u, n // 4] % 4
                        mm = pe.matmul(o_ps[:, hh * HD:(hh + 1) * HD],
                                       prob_t[w][:, (n % 4) * P:(n % 4 + 1) * P], v_tile(u, t, hh),
                                       start=(n == mine[0][0]), stop=(n == mine[-1][0]))
                mm.then_inc(pv_done, 1)

            def transpose_y(i):
                pe.wait_ge(o_scaled, i + 1)
                for h in range(2):
                    n, bank = bank_of(narrow, plan.narrow, ("y", i, h))
                    if n >= 2:
                        pe.wait_ge(narrow_read[n % 2], n // 2)
                    for j in range(4):
                        f = 4 * h + j
                        t = pe.transpose(bank[:, j * P:(j + 1) * P], qo[:, i, f * P:(f + 1) * P], ident[:, :])
                    t.then_inc(narrow_full, 1)

            def out_products(i, share, shares):
                passes = [(y_hi[:, i, k, :], wo_hi, k) for k in range(FT)] + \
                         [(y_hi[:, i, k, :], wo_lo, k) for k in range(FT)] + \
                         [(y_lo[:, k, i * P:(i + 1) * P], wo_hi, k) for k in range(FT)]
                total = 2 * len(passes)
                for n in range(share * total // shares, (share + 1) * total // shares):
                    half, p = divmod(n, len(passes))
                    if n == 0:
                        pe.wait_ge(y_split, i + 1)
                        pe.wait_ge(wo_split, FT)
                    if p == 0 and i == 0:
                        pe.wait_ge(gate_done, GATES - 1 + half)
                    if p == 0 and i > 0:
                        pe.wait_ge(res_sum, 2 * i + half - 1)
                    y, w, k = passes[p]
                    mm = pe.matmul(long_ps[half][:, :], y, w[:, k, half * HALF:(half + 1) * HALF],
                                   start=(p == 0), stop=(p == len(passes) - 1))
                    if p == len(passes) - 1:
                        mm.then_inc(out_full, 1)

            def filler(v, part):
                if v < GATE_ITERATIONS * GATES:
                    gate_products(v, part)
                for i in range(NB):
                    if OUT_AT[i] <= v < OUT_AT[i] + OUT_ITERATIONS[i]:
                        out_products(i, 2 * (v - OUT_AT[i]) + part, 2 * OUT_ITERATIONS[i])

            filler(0, 0)
            transpose_q(0)
            for v in range(ITERATIONS):
                if 0 <= v - 1 < n_units:
                    score(v - 1)
                if 0 <= v - 2 < n_units:
                    transpose_probs(v - 2)
                if v:
                    filler(v, 0)
                if v + 1 < n_units:
                    transpose_q(v + 1)
                filler(v, 1)
                if 0 <= v - 3 < n_units:
                    times_v(v - 3)
                if block_at(v, Y_AT) is not None:
                    transpose_y(block_at(v, Y_AT))

        @block.scalar
        def _(act):
            nc.scalar.preload_act_table_set("natural_log_exp_and_others")

            def chunk_hi(c):
                s = slot_of(c)
                for h in range(2):
                    act.wait_ge(chunk_in[s][h], 16 * (c // 3 + 1))
                    k = slice(h * KT // 2, (h + 1) * KT // 2)
                    act.activation(w_hi[s][:, k, :], w_raw[s][:, k, :], ACT.Copy).then_inc(chunk_rounded, 1)

            def rows_hi(r):
                for h in range(2):
                    act.wait_ge(narrow_full, plan.narrow["rows", r, h] + 1)
                    _, bank = bank_of(narrow, plan.narrow, ("rows", r, h))
                    dst, i = (mem_hi, r) if r < NBM else (x_hi, r - NBM)
                    act.activation(dst[:, 4 * h:4 * h + 4, i * P:(i + 1) * P],
                                   bank[:, :].rearrange("p (k t) -> p k t", k=4), ACT.Copy)\
                       .then_inc(rows_rounded, 1)

            def keys_hi(k):
                dst, heads = key_dst(k)
                act.wait_ge(narrow_full, plan.narrow["keys", k] + 1)
                _, bank = bank_of(narrow, plan.narrow, ("keys", k))
                act.activation(dst, bank[:, 0:heads * P].rearrange("p (h t) -> p h t", h=heads), ACT.Copy)\
                   .then_inc(keys_rounded, 1)

            def gate_hi(f):
                act.wait_ge(gate_in[f % 2], 16 * (f // 2 + 1))
                act.activation(g_hi[f % 2][:, :, :], g_raw[f % 2][:, :, :], ACT.Copy).then_inc(gate_rounded, 1)

            split_at = {0: -1, 1: 0, 2: 1}
            for c in range(3, len(kinds)):
                split_at[c] = plan.last_job[c - 1] - 4
            chunk_hi(0)
            for what, n in plan.steps:
                if what == "rows":
                    rows_hi(n)
                elif what == "keys":
                    keys_hi(n)
                else:
                    for c, job in split_at.items():
                        if job == n:
                            chunk_hi(c)
                    if n == n_jobs - 4:
                        gate_hi(0)
                    if n == n_jobs - 3:
                        gate_hi(1)

            def half_sigmoid(n):
                e = gate_e[n % 2][:, :]
                if n >= 2:
                    act.wait_ge(gate_done, n - 1)
                act.wait_ge(gate_full, n + 1)
                act.activation(e, long_ps[n % 2][:, :], ACT.Exp, bias=neg_z_bias[:, n // 2:n // 2 + 1], scale=-1.0)\
                   .then_inc(gate_exp, 1)
                act.wait_ge(gate_exp, n + 1)
                act.activation(e, e, ACT.Ln, bias=1.0).then_inc(gate_logged, 1)
                act.wait_ge(gate_logged, n + 1)
                act.activation(e, e, ACT.Exp, scale=-1.0).then_inc(gate_sigmoid, 1)

            def unit_q_hi(u):
                heads = UNITS[u][3]
                act.wait_ge(narrow_full, plan.narrow["q", u] + 1)
                _, bank = bank_of(narrow, plan.narrow, ("q", u))
                if u >= QS:
                    act.wait_ge(wide_full, scores_turn(u - QS) + 1)
                act.activation(q_hi[u % QS][:, 0:heads * P], bank[:, 0:heads * P], ACT.Copy, scale=SCALE)\
                   .then_inc(q_rounded, 1)

            def unit_exp(u):
                kind, _, _, heads, nk = UNITS[u]
                s, r = u % 2, u % 4
                act.wait_ge(neg_max, u + 1)
                if kind == "c":
                    _, bank = bank_of(wide, plan.wide, ("scores", u, 0))
                    if u >= 2:
                        act.wait_ge(narrow_full, probs_turn(u - 2) + 1)
                if u >= 4:
                    act.wait_ge(o_done, u - 3)
                for hh in range(heads):
                    cols = slice(hh * C, hh * C + nk * P)
                    src = bank[:, cols] if kind == "c" else prob[s][:, cols]
                    e = act.activation(prob[s][:, cols], src, ACT.Exp, bias=nb[:, r, hh:hh + 1],
                                       accum_out=den[:, r, hh:hh + 1])
                e.then_inc(probs_ready, 1)
                if kind == "a":
                    act.wait_ge(sink_gap_ready, a_index[u] + 1)
                    act.activation(gap_exp[:, r, :], gap[:, r, :], ACT.Exp).then_inc(sink_exp_ready, 1)

            def unit_pt(u):
                for c, w in plan.pt_chunks(u):
                    if w % 2 == 0:
                        act.wait_ge(narrow_full, plan.narrow["probs", u, c] + 1)
                        n, bank = bank_of(narrow, plan.narrow, ("probs", u, c))
                        if w >= 4:
                            act.wait_ge(pv_done, plan.pt_unit[w - 4] + 1)
                        size = P * len(prob_tiles(u)[4 * c:4 * c + 4])
                        act.activation(prob_t[w % 4][:, 0:size], bank[:, 0:size], ACT.Copy).then_inc(narrow_read[n % 2], 1)

            def block_rms(i):
                act.wait_ge(o_done, UB * (i + 1))
                if i == 0:
                    act.wait_ge(gate_done, GATES)
                for j, (lo, n) in enumerate(((0, W_A), (W_A, W_B), (W_A + W_B, W_C))):
                    sqr = act.activation(square_out[:, lo:lo + n], qo[:, i, lo:lo + n], ACT.Square, scale=float(n) ** -0.5,
                                         accum_out=sq[:, i % 2, j:j + 1])
                sqr.then_inc(squares, 1)
                act.wait_ge(squares, i + 1)
                act.activation(rms_log[:, i % 2, :], sq[:, i % 2, :], ACT.Ln, bias=RMS_EPS).then_inc(rms_logged, 1)
                act.wait_ge(rms_logged, i + 1)
                act.activation(rms[:, i % 2, :], rms_log[:, i % 2, :], ACT.Exp, scale=-0.5).then_inc(rms_ready, 1)

            act.wait_ge(negated, 2)
            unit_q_hi(0)
            for v in range(ITERATIONS):
                if 0 <= v - 2 < n_units:
                    unit_pt(v - 2)
                if 0 <= v - 1 < n_units:
                    unit_exp(v - 1)
                if v + 1 < n_units:
                    unit_q_hi(v + 1)
                if v % GATE_ITERATIONS == GATE_ITERATIONS - 1 and v < GATE_ITERATIONS * GATES:
                    half_sigmoid(v // GATE_ITERATIONS)
                f, since = divmod(v, 2 * GATE_ITERATIONS)
                if since == GATE_ITERATIONS and 1 <= f < FT - 1:
                    gate_hi(f + 1)
                for k in wo_tiles(v):
                    act.wait_ge(gate_cols_in, 32)
                    act.wait_ge(wo_in[k], 16)
                    act.activation(wo_hi[:, k, :], wo_raw[:, k, :], ACT.Copy, scale=g_col[:, k:k + 1])\
                       .then_inc(wo_rounded, 1)
                i = block_at(v, RMS_AT)
                if i is not None:
                    block_rms(i)
                i = block_at(v, YSPLIT_AT)
                if i is not None:
                    n = plan.narrow["y", i, 1]
                    act.wait_ge(narrow_read[n % 2], n // 2 + 1)
                    act.activation(y_hi[:, i, :, :], zt[:, :, i * P:(i + 1) * P], ACT.Copy).then_inc(y_rounded, 1)
                i = block_at(v, STATS_AT)
                if i is not None:
                    s = i % 2
                    act.wait_ge(ln_stats, i + 1)
                    act.activation(ln_log[:, s:s + 1], moments[:, s, 1:2], ACT.Ln, bias=LN_EPS).then_inc(ln_logged, 1)
                    act.wait_ge(ln_logged, i + 1)
                    act.activation(ln_rstd[:, s:s + 1], ln_log[:, s:s + 1], ACT.Exp, scale=-0.5)\
                       .then_inc(ln_rstd_ready, 1)
                i = block_at(v, NORM_AT)
                if i is not None:
                    s = i % 2
                    act.wait_ge(ln_shift_ready, i + 1)
                    act.activation(res[s][:, :], res[s][:, :], ACT.Identity, bias=ln_shift[:, s:s + 1],
                                   scale=ln_rstd[:, s:s + 1]).then_inc(normed, 1)

        @block.vector
        def _(dve):
            def rows_lo(r):
                for h in range(2):
                    dve.wait_ge(rows_rounded, 2 * r + h + 1)
                    n, bank = bank_of(narrow, plan.narrow, ("rows", r, h))
                    hi, lo, i = (mem_hi, mem_lo, r) if r < NBM else (x_hi, x_lo, r - NBM)
                    ks, cols = slice(4 * h, 4 * h + 4), slice(i * P, (i + 1) * P)
                    dve.tensor_tensor(lo[:, ks, cols], bank[:, :].rearrange("p (k t) -> p k t", k=4),
                                      f32(hi[:, ks, cols]), ALU.subtract).then_inc(narrow_read[n % 2], 1)

            def keys_lo(k):
                dst, heads = key_dst(k)
                dve.wait_ge(keys_rounded, k + 1)
                n, bank = bank_of(narrow, plan.narrow, ("keys", k))
                dve.tensor_tensor(dst[HD:P], bank[HD:P, 0:heads * P].rearrange("p (h t) -> p h t", h=heads),
                                  f32(dst[HD:P]), ALU.subtract).then_inc(narrow_read[n % 2], 1)

            rotations = [0]

            def finish_job(n):
                c, i = jobs[n]
                kind, of_mem, col, q_col = kinds[c]
                dve.wait_ge(wide_full, plan.wide["job", n] + 1)
                _, bank = bank_of(wide, plan.wide, ("job", n))
                if n == NBM * 2:
                    dve.wait_ge(bias_in, 16)
                    dve.wait_ge(rope_in, 16)
                k = plan.key_jobs.index(n) if n in plan.key_jobs else None
                if k is not None and k >= 2:
                    dve.wait_ge(narrow_full, plan.narrow["keys", k - 2] + 1)
                if kind == "mk":
                    dve.tensor_copy(keys2[k % 2][:, :, :, :],
                                    heads_view(bank[:, 0:C], HC).unsqueeze(2).to_broadcast([P, HC, 2, HD]))\
                       .then_inc(h_read, 1)
                elif kind == "mv":
                    dve.tensor_copy(v_c[:, i, :], bank[:, 0:C]).then_inc(h_read, 1)
                else:
                    b = b_row[:, col:col + C]
                    dst = {"vb": v_b[:, i, :], "qc": qo[:, i, q_col:q_col + C] if q_col is not None else None}\
                        .get(kind, h_sb[:, :])
                    if kind == "kva":
                        dve.tensor_tensor(v_a[:, i, :], bank[:, W_KV:C], b[:, W_KV:C], ALU.add)
                        dst, b = h_sb[:, 0:W_KV], b[:, 0:W_KV]
                    dve.tensor_tensor(dst, bank[:, 0:b.shape[1]], b, ALU.add).then_inc(h_read, 1)
                if kind in ("kva", "kb", "q"):
                    m = rotations[0]
                    rotations[0] += 1
                    width = W_KV if kind == "kva" else C
                    nh = width // HD
                    dve.wait_ge(h_read, n + 1)
                    h3 = heads_view(h_sb[:, 0:width], nh)
                    r3, s3 = heads_view(rot_cos[:, 0:width], nh), heads_view(rot_sin[:, 0:width], nh)
                    tab = rope[:, i, :]

                    def per_head(lo, hi):
                        return tab[:, lo:hi].unsqueeze(1).to_broadcast([P, nh, hi - lo])

                    half = HD // 2
                    dve.tensor_tensor(r3, h3, per_head(0, HD), ALU.mult)
                    dve.tensor_tensor(s3[:, :, 0:half], h3[:, :, half:HD], per_head(HD, HD + half), ALU.mult)
                    dve.tensor_tensor(s3[:, :, half:HD], h3[:, :, 0:half], per_head(HD + half, 2 * HD), ALU.mult)\
                       .then_inc(rope_parts, 1)
                    dve.wait_ge(rope_parts, m + 1)
                    if k is not None:
                        shape = [P, nh, 2, HD]
                        dve.tensor_tensor(keys2[k % 2][:, 0:nh, :, :], r3.unsqueeze(2).to_broadcast(shape),
                                          s3.unsqueeze(2).to_broadcast(shape), ALU.add).then_inc(keys_rotated, 1)
                    else:
                        dve.tensor_tensor(qo[:, i, q_col:q_col + C], rot_cos[:, :], rot_sin[:, :], ALU.add)\
                           .then_inc(q_rotated, 1)

            for what, n in plan.steps:
                {"rows": rows_lo, "job": finish_job, "keys": keys_lo}[what](n)

            dve.wait_ge(gate_cols_in, 32)
            dve.wait_ge(sinks_in, 16)
            dve.tensor_scalar(neg_z_bias[:, :], z_bias[:, :], -1.0, None, ALU.mult).then_inc(negated, 1)
            dve.tensor_scalar(neg_sink[:, :], sink_row[:, :], -1.0, None, ALU.mult).then_inc(negated, 1)

            def half_silu(n):
                f, h = divmod(n, 2)
                dve.wait_ge(gate_sigmoid, n + 1)
                dve.scalar_tensor_tensor(zt[:, f, h * HALF:(h + 1) * HALF], long_ps[n % 2][:, :], z_bias[:, f:f + 1],
                                         gate_e[n % 2][:, :], ALU.add, ALU.mult).then_inc(gate_done, 1)

            def unit_q_lo(u):
                heads = UNITS[u][3]
                dve.wait_ge(q_rounded, u + 1)
                n, bank = bank_of(narrow, plan.narrow, ("q", u))
                if u >= QS:
                    dve.wait_ge(wide_full, scores_turn(u - QS) + 1)
                dve.scalar_tensor_tensor(q_lo[u % QS][:, 0:heads * P], bank[:, 0:heads * P], SCALE,
                                         f32(q_hi[u % QS][:, 0:heads * P]), ALU.mult, ALU.subtract)\
                   .then_inc(narrow_read[n % 2], 1)

            def unit_max(u):
                kind, i, h0, heads, nk = UNITS[u]
                s, r = u % 2, u % 4
                if u >= 4:
                    dve.wait_ge(probs_ready, u - 3)
                if kind == "c":
                    dve.wait_ge(wide_full, plan.wide["scores", u, 0] + 1)
                    _, bank = bank_of(wide, plan.wide, ("scores", u, 0))
                    dve.tensor_reduce(nb[:, r, :], heads_view(bank[:, 0:2 * C], 2), AX.X, ALU.max, negate=True)\
                       .then_inc(neg_max, 1)
                    return
                if u >= 2:
                    dve.wait_ge(narrow_full, probs_turn(u - 2) + 1)
                for c, (lo, hi) in enumerate(key_chunks(u)):
                    dve.wait_ge(wide_full, plan.wide["scores", u, c] + 1)
                    _, bank = bank_of(wide, plan.wide, ("scores", u, c))
                    if kind == "b":
                        off = (NB - nk) * P
                        ttr = dve.tensor_tensor_reduce(prob[s][:, lo:hi], bank[:, 0:hi - lo],
                                                       mask_b[:, off + lo:off + hi], 1.0, -3e38, ALU.add, ALU.max,
                                                       mx[:, s, c:c + 1])
                    else:
                        for hh in range(heads):
                            cols = slice(hh * C, hh * C + nk * P)
                            ttr = dve.tensor_tensor_reduce(prob[s][:, cols], bank[:, cols],
                                                           mask_a[:, (2 - nk) * P:2 * P], 1.0, -3e38, ALU.add,
                                                           ALU.max, mx[:, s, hh:hh + 1])
                ttr.then_inc(row_max, 1)
                dve.wait_ge(row_max, masked_index[u] + 1)
                if kind == "b":
                    dve.tensor_reduce(nb[:, r, 0:1], mx[:, s, 0:len(key_chunks(u))], AX.X, ALU.max, negate=True)\
                       .then_inc(neg_max, 1)
                else:
                    ns = neg_sink[:, h0:h0 + 2]
                    dve.scalar_tensor_tensor(nb[:, r, :], mx[:, s, :], -1.0, ns, ALU.mult, ALU.min)\
                       .then_inc(neg_max, 1)
                    dve.wait_ge(neg_max, u + 1)
                    dve.tensor_tensor(gap[:, r, :], nb[:, r, :], ns, ALU.subtract).then_inc(sink_gap_ready, 1)

            def unit_pt(u):
                for c, w in plan.pt_chunks(u):
                    if w % 2 == 1:
                        dve.wait_ge(narrow_full, plan.narrow["probs", u, c] + 1)
                        n, bank = bank_of(narrow, plan.narrow, ("probs", u, c))
                        if w >= 4:
                            dve.wait_ge(pv_done, plan.pt_unit[w - 4] + 1)
                        size = P * len(prob_tiles(u)[4 * c:4 * c + 4])
                        dve.tensor_copy(prob_t[w % 4][:, 0:size], bank[:, 0:size]).then_inc(narrow_read[n % 2], 1)

            def unit_out(u):
                kind, i, _, heads, _ = UNITS[u]
                r = u % 4
                dve.wait_ge(probs_ready, u + 1)
                total = den
                if kind == "a":
                    dve.wait_ge(sink_exp_ready, a_index[u] + 1)
                    dve.tensor_tensor(den_all[:, r, :], den[:, r, :], gap_exp[:, r, :], ALU.add)\
                       .then_inc(den_sum, 1)
                    dve.wait_ge(den_sum, a_index[u] + 1)
                    total = den_all
                dve.reciprocal(rden[:, r, 0:heads], total[:, r, 0:heads]).then_inc(den_rcp, 1)
                dve.wait_ge(den_rcp, u + 1)
                dve.wait_ge(pv_done, u + 1)
                col = q_cols(u, 0)
                dve.tensor_tensor(heads_view(qo[:, i, col:col + heads * HD], heads),
                                  heads_view(o_ps[:, 0:heads * HD], heads),
                                  rden[:, r, 0:heads].unsqueeze(2).to_broadcast([P, heads, HD]), ALU.mult)\
                   .then_inc(o_done, 1)

            dve.wait_ge(negated, 2)
            dve.wait_ge(masks_in, 32)
            unit_q_lo(0)
            for v in range(ITERATIONS):
                if 0 <= v - 4 < n_units:
                    unit_out(v - 4)
                if v % GATE_ITERATIONS == 0 and 0 < v <= GATE_ITERATIONS * GATES:
                    half_silu(v // GATE_ITERATIONS - 1)
                if 0 <= v - 1 < n_units:
                    unit_max(v - 1)
                if 0 <= v - 2 < n_units:
                    unit_pt(v - 2)
                if v + 1 < n_units:
                    unit_q_lo(v + 1)
                for half in range(2):
                    i = block_at(v, RES_AT[half])
                    if i is not None:
                        cols = slice(half * HALF, (half + 1) * HALF)
                        dve.wait_ge(res_in[i % 2], 16 * (i // 2 + 1))
                        dve.wait_ge(out_full, 2 * i + half + 1)
                        dve.scalar_tensor_tensor(res[i % 2][:, cols], res[i % 2][:, cols], ALPHA, long_ps[half][:, :],
                                                 ALU.mult, ALU.add).then_inc(res_sum, 1)
                for k in wo_tiles(v):
                    dve.wait_ge(wo_rounded, k + 1)
                    dve.scalar_tensor_tensor(wo_lo[:, k, :], wo_raw[:, k, :], g_col[:, k:k + 1], f32(wo_hi[:, k, :]),
                                             ALU.mult, ALU.subtract).then_inc(wo_split, 1)
                i = block_at(v, SCALE_AT)
                if i is not None:
                    dve.wait_ge(rms_ready, i + 1)
                    for j, (lo, n) in enumerate(((0, W_A), (W_A, W_B), (W_A + W_B, W_C))):
                        ts = dve.tensor_scalar(qo[:, i, lo:lo + n], qo[:, i, lo:lo + n], rms[:, i % 2, j:j + 1], None,
                                               ALU.mult)
                    ts.then_inc(o_scaled, 1)
                i = block_at(v, Y_AT)
                if i is not None:
                    for h in range(2):
                        dve.wait_ge(narrow_full, plan.narrow["y", i, h] + 1)
                        n, bank = bank_of(narrow, plan.narrow, ("y", i, h))
                        z = zt[:, 4 * h:4 * h + 4, i * P:(i + 1) * P]
                        dve.tensor_tensor(z, bank[:, :].rearrange("p (f t) -> p f t", f=4), z, ALU.mult)\
                           .then_inc(narrow_read[n % 2], 1)
                i = block_at(v, STATS_AT)
                if i is not None:
                    s = i % 2
                    dve.wait_ge(res_sum, 2 * i + 2)
                    for h in range(2):
                        bs = dve.bn_stats(stats[:, s, h, :], res[s][:, h * HALF:(h + 1) * HALF])
                    bs.then_inc(ln_part, 1)
                    dve.wait_ge(ln_part, i + 1)
                    dve.bn_aggr(moments[:, s, :], stats[:, s, :, :]).then_inc(ln_stats, 1)
                i = block_at(v, NORM_AT)
                if i is not None:
                    s = i % 2
                    dve.wait_ge(ln_rstd_ready, i + 1)
                    dve.scalar_tensor_tensor(ln_shift[:, s:s + 1], moments[:, s, 0:1], -1.0, ln_rstd[:, s:s + 1],
                                             ALU.mult, ALU.mult).then_inc(ln_shift_ready, 1)

        @block.gpsimd
        def _(pool):
            for c in range(len(kinds)):
                s = slot_of(c)
                for h in range(2):
                    pool.wait_ge(chunk_rounded, 2 * c + h + 1)
                    k = slice(h * KT // 2, (h + 1) * KT // 2)
                    pool.tensor_tensor(w_lo[s][:, k, :], w_raw[s][:, k, :], f32(w_hi[s][:, k, :]), ALU.subtract)\
                        .then_inc(chunk_split, 1)
            def gate_lo(f):
                pool.wait_ge(gate_rounded, f + 1)
                pool.tensor_tensor(g_lo[f % 2][:, :, :], g_raw[f % 2][:, :, :], f32(g_hi[f % 2][:, :, :]),
                                   ALU.subtract).then_inc(gate_split, 1)

            gate_lo(0)
            gate_lo(1)

            def unit_q_twice(u):
                _, i, _, heads, _ = UNITS[u]
                if u >= Q2:
                    pool.wait_ge(narrow_full, plan.narrow["q", u - Q2] + 1)
                q = heads_view(qo[:, i, q_cols(u, 0):q_cols(u, 0) + heads * HD], heads)
                pool.tensor_copy(q2[u % Q2][:, 0:heads, :, :], q.unsqueeze(2).to_broadcast([P, heads, 2, HD]))\
                    .then_inc(q_twice, 1)

            pool.wait_ge(q_rotated, 3 * NB)
            pool.wait_ge(h_read, n_jobs)
            for u in range(Q2 - 1):
                unit_q_twice(u)
            for v in range(ITERATIONS):
                if v + Q2 - 1 < n_units:
                    unit_q_twice(v + Q2 - 1)
                f, since = divmod(v, 2 * GATE_ITERATIONS)
                if since == GATE_ITERATIONS and 1 <= f < FT - 1:
                    gate_lo(f + 1)
                i = block_at(v, YSPLIT_AT)
                if i is not None:
                    pool.wait_ge(y_rounded, i + 1)
                    cols = slice(i * P, (i + 1) * P)
                    pool.tensor_tensor(y_lo[:, :, cols], zt[:, :, cols], f32(y_hi[:, i, :, :]), ALU.subtract)\
                        .then_inc(y_split, 1)
                i = block_at(v, NORM_AT)
                if i is not None:
                    s = i % 2
                    if i == 0:
                        pool.wait_ge(ln_in, 32)
                    pool.wait_ge(normed, i + 1)
                    pool.tensor_tensor(res[s][:, :], res[s][:, :], gain[:, :], ALU.mult).then_inc(gained, 1)
                    pool.wait_ge(gained, i + 1)
                    pool.tensor_tensor(res[s][:, :], res[s][:, :], bias[:, :], ALU.add).then_inc(finished, 1)


def rope_table():
    pos = np.arange(SEQ, dtype=np.float32)
    inv = np.float32(10000.0) ** (-np.arange(0, HD, 2, dtype=np.float32) / np.float32(HD))
    ang = pos[:, None] * inv[None, :].astype(np.float32)
    c, s = np.cos(ang), np.sin(ang)
    return np.concatenate([c, c, -s, s], axis=1).astype(np.float32)


def masks():
    p = np.arange(P)[:, None]
    d = p + P - np.arange(2 * P)[None, :]
    a = np.where((d >= 0) & (d < WINDOW), 0.0, MASKED).astype(np.float32)
    d = p + (NB - 1) * P - np.arange(SEQ)[None, :]
    count = sum(((d >= 0) & (d <= w) & (d % r == 0)).astype(np.float64) for w, r in PAIRS)
    b = np.where(count > 0, np.log(np.maximum(count, 1.0)), MASKED).astype(np.float32)
    return a, b


_INS = ["x", "mem", "w_in", "b_in", "w_mem", "attn_sinks", "g_branch", "w_out", "ln_gain", "ln_bias"]


def kernel(**inputs):
    import concourse.bacc as bacc
    from concourse.bass_utils import run_bass_kernel_spmd

    nc = bacc.Bacc("TRN2", target_bir_lowering=False, num_devices=1, dynamic_dma_scratch_size=1024)
    mask_a, mask_b = masks()
    arrays = {name: np.ascontiguousarray(inputs[name]) for name in _INS}
    arrays |= {"ident": np.eye(P, dtype=np.float32), "rope": rope_table(), "mask_a": mask_a, "mask_b": mask_b}
    arrays = {f"in_{name}": a for name, a in arrays.items()}
    args = [nc.dram_tensor(name, a.shape, mybir.dt.from_np(a.dtype), kind="ExternalInput").ap()
            for name, a in arrays.items()]
    out = nc.dram_tensor("out", (1, SEQ, DM), F32, kind="ExternalOutput").ap()
    layer(nc, *args, out)
    r = run_bass_kernel_spmd(nc, [arrays], core_ids=[0])
    return r.results[0]["out"]
```

```python
from contextlib import ExitStack

import numpy as np

import concourse.bass as bass
from concourse import mybir

F32 = mybir.dt.float32
F32R = mybir.dt.float32r
ALU = mybir.AluOpType
ACT = mybir.ActivationFunctionType
AX = mybir.AxisListType

P = 128
SEQ = 1024
DM = 1024
MEM = 256
NB = SEQ // P
NBM = MEM // P
KT = DM // P
HD = 64
HA, GA = 8, 2
HB = 4
HC = 4
WINDOW = 128
PAIRS = ((128, 1), (512, 4), (2048, 16))
DEPTH = 1
ALPHA = float((2 * DEPTH) ** 0.25)
RMS_EPS = 1e-6
LN_EPS = 1e-5
SCALE = HD ** -0.5
MASKED = -1e30
C = 256
HALF = 512
POOL_COLS = 320

W_A, W_KV, W_B, W_C = HA * HD, GA * HD, HB * HD, HC * HD
COL_QA, COL_KA, COL_VA = 0, W_A, W_A + W_KV
COL_QB = COL_VA + W_KV
COL_KB, COL_VB = COL_QB + W_B, COL_QB + 2 * W_B
COL_QC = COL_VB + W_B
COL_Z = COL_QC + W_C
QKV = COL_Z
FT = (W_A + W_B + W_C) // P


def chunks():
    return [("kva", False, COL_KA, None), ("kb", False, COL_KB, None), ("vb", False, COL_VB, None),
            ("mk", True, 0, None), ("mv", True, W_C, None),
            ("q", False, COL_QA, 0), ("q", False, COL_QA + C, C), ("q", False, COL_QB, W_A),
            ("qc", False, COL_QC, W_A + W_B)]


def units():
    out = []
    for i in range(NB):
        window = min(i + 1, 2)
        a = [("a", i, 2 * j, 2, window) for j in range(HA // 2)]
        b = [("b", i, j, 1, i + 1) for j in range(HB)]
        c = [("c", i, 2 * j, 2, NBM) for j in range(HC // 2)]
        if i < NB - 1:
            out += [c[0], b[0], a[3], b[1], a[2], b[3], a[1], b[2], a[0], c[1]]
        else:
            out += [a[0], b[0], a[1], b[2], a[2], b[3], a[3], b[1], c[0], c[1]]
    return out


UNITS = units()
UB = len(UNITS) // NB
GATE_ITERATIONS = 2
RS = 4
QS = 3
Q2 = 3
GATES = 2 * FT
LAST_TILE_AT = 2 * GATE_ITERATIONS * (FT - 1)
WO_AT = [LAST_TILE_AT + at for at in (1, 2, 2, 3, 3, 4, 6, 8)]
BRANCHES = ((0, W_A), (W_A, W_B), (W_A + W_B, W_C))
BRANCH_TILES = [list(range(lo // P, (lo + n) // P)) for lo, n in BRANCHES]
OUT_ITERATIONS = (7, 7, 7, 7, 8, 9, 5, 4)
OUT_AT = [LAST_TILE_AT + 5]
for i in range(1, NB):
    OUT_AT.append(max(OUT_AT[-1] + OUT_ITERATIONS[i - 1], UB * (i + 1) + (6 if i < NB - 1 else 1)))


def branch_done(i, j):
    return max(u for u, unit in enumerate(UNITS) if unit[0] == "abc"[j] and unit[1] == i) + 4


RMS_AT = {(i, j): max(OUT_AT[i] - 6 + j, branch_done(i, j)) for i in range(1, NB - 1) for j in range(3)}
RMS_AT.update({(0, j): OUT_AT[0] - before for j, before in enumerate((7, 4, 0))})
RMS_AT.update({(NB - 1, j): branch_done(NB - 1, j) for j in range(3)})
SCALE_AT = {key: v if key[0] == NB - 1 else v + 1 for key, v in RMS_AT.items()}
Y_AT = {key: v + 1 for key, v in SCALE_AT.items()}
YSPLIT_AT = {key: v if key[0] == NB - 1 else v + 2 for key, v in Y_AT.items()}
BY_BRANCH = (0, NB - 1)
RES_AT = [{i: OUT_AT[i] + (n if i in BY_BRANCH else -(-n // 2)) - 1 for i, n in enumerate(OUT_ITERATIONS)},
          {i: OUT_AT[i] + n for i, n in enumerate(OUT_ITERATIONS)}]
STATS_AT = RES_AT[1]
NORM_AT = {i: v + 1 for i, v in RES_AT[1].items()}
NORM_AT[NB - 2] = YSPLIT_AT[NB - 1, 2]
for table in (RMS_AT, SCALE_AT, Y_AT, YSPLIT_AT, NORM_AT):
    assert [table[key] for key in sorted(table)] == sorted(table.values())
ITERATIONS = max(NORM_AT.values()) + 1


def halves_at(v):
    n, step = divmod(v, GATE_ITERATIONS)
    if v in (LAST_TILE_AT + 3, LAST_TILE_AT + 4):
        return [v - LAST_TILE_AT - 3 + GATES - 2]
    return [n] if step == GATE_ITERATIONS - 1 and 0 <= n < GATES - 2 else []


def stage_at(v, table):
    return [key for key, at in sorted(table.items()) if at == v]


def wo_tiles(v):
    return [k for k in range(FT) if WO_AT[k] == v]


def out_order(i):
    halves_of = [[0, 1]] if i in BY_BRANCH else [[0], [1]]
    return [(half, k, p) for halves in halves_of for tiles in BRANCH_TILES
            for half in halves for k in tiles for p in range(3)]


def key_chunks(u):
    kind, _, _, heads, nk = UNITS[u]
    if kind != "b":
        return [(0, C * (heads - 1) + nk * P)]
    return [(c, min(c + HALF, nk * P)) for c in range(0, nk * P, HALF)]


def prob_tiles(u):
    kind, i, _, heads, nk = UNITS[u]
    if kind == "b":
        return [(0, t, t * P) for t in range(nk)]
    first = i + 1 - nk if kind == "a" else 0
    return [(hh, first + t, hh * C + t * P) for hh in range(heads) for t in range(nk)]


class Plan:

    def __init__(self):
        self.chunks = chunks()
        self.jobs = [(c, i) for c, (_, of_mem, _, _) in enumerate(self.chunks)
                     for i in range(NBM if of_mem else NB)]
        self.last_job = {c: max(n for n, j in enumerate(self.jobs) if j[0] == c)
                         for c in range(len(self.chunks))}
        self.key_jobs = [n for n, (c, _) in enumerate(self.jobs)
                         if self.chunks[c][0] in ("mk", "kva", "kb")]
        self.steps = [("rows", 0), ("rows", 1)]
        for n in range(len(self.jobs)):
            if n and n + 1 < NB + NBM:
                self.steps.append(("rows", n + 1))
            self.steps.append(("job", n))
            if n - 1 in self.key_jobs:
                self.steps.append(("keys", self.key_jobs.index(n - 1)))
        wide, narrow = [], []
        for what, n in self.steps:
            if what != "rows":
                (narrow if what == "keys" else wide).append((what, n))
        self.pt_unit = []
        self.pt = {}
        narrow.append(("q", 0))
        for v in range(ITERATIONS):
            if 0 <= v - 1 < len(UNITS):
                wide += [("scores", v - 1, c) for c in range(len(key_chunks(v - 1)))]
            if 0 <= v - 2 < len(UNITS):
                for c in range(-(-len(prob_tiles(v - 2)) // 4)):
                    self.pt[v - 2, c] = len(self.pt_unit)
                    self.pt_unit.append(v - 2)
                    narrow.append(("probs", v - 2, c))
            narrow += [("y", i, j) for i, j in stage_at(v, Y_AT)]
            if v + 1 < len(UNITS):
                narrow.append(("q", v + 1))
        self.wide = {key: n for n, key in enumerate(wide)}
        self.narrow = {key: n for n, key in enumerate(narrow)}
        for n, key in enumerate(wide):
            assert key[0] != "scores" or wide[n - 3][0] == "job" or wide[n - 3][1] <= key[1] - 2

    def pt_chunks(self, u):
        return [(c, self.pt[u, c]) for c in range(-(-len(prob_tiles(u)) // 4))]


def layer(nc, x, mem, w_in, b_in, w_mem, sinks, g_branch, w_out, ln_gain, ln_bias,
          ident_d, rope_d, mask_a_d, mask_b_d, out):
    plan = Plan()
    jobs, kinds = plan.jobs, plan.chunks
    n_jobs, n_units = len(jobs), len(UNITS)

    with ExitStack() as ctx:
        def sem(name):
            return ctx.enter_context(nc.semaphore(name))

        ident_in, bias_in, rope_in = sem("ident_in"), sem("bias_in"), sem("rope_in")
        gate_cols_in, sinks_in, masks_in = sem("gate_cols_in"), sem("sinks_in"), sem("masks_in")
        wo_in, ln_in = [sem(f"wo_in{k}") for k in range(FT)], sem("ln_in")
        bias_first_in, rope_first_in = sem("bias_first_in"), sem("rope_first_in")
        rows_in = [[sem(f"rows_in{s}{h}") for h in range(2)] for s in range(RS)]
        chunk_in = [[sem(f"chunk_in{s}{h}") for h in range(2)] for s in range(3)]
        gate_in = [sem(f"gate_in{s}") for s in range(2)]
        res_in = [sem(f"res_in{s}") for s in range(2)]
        stored = [sem(f"stored{s}") for s in range(2)]
        wide_full, narrow_full = sem("wide_full"), sem("narrow_full")
        gate_full, x_used, out_full = sem("gate_full"), sem("x_used"), sem("out_full")
        narrow_read = [sem(f"narrow_read{b}") for b in range(2)]
        rows_rounded, chunk_rounded, chunk_split = sem("rows_rounded"), sem("chunk_rounded"), sem("chunk_split")
        first_split = sem("first_split")
        rows_full, rows_split = sem("rows_full"), [sem(f"rows_split{h}") for h in range(2)]
        gate_rounded, gate_split, h_read = sem("gate_rounded"), sem("gate_split"), sem("h_read")
        rope_parts, keys_rotated, q_rotated = sem("rope_parts"), sem("keys_rotated"), sem("q_rotated")
        keys_rounded, negated, gate_exp = sem("keys_rounded"), sem("negated"), sem("gate_exp")
        gate_logged, gate_sigmoid, gate_done = sem("gate_logged"), sem("gate_sigmoid"), sem("gate_done")
        q_twice, q_rounded, row_max = sem("q_twice"), sem("q_rounded"), sem("row_max")
        neg_max, sink_gap_ready, sink_exp_ready = sem("neg_max"), sem("sink_gap_ready"), sem("sink_exp_ready")
        probs_ready, pv_done, den_sum = sem("probs_ready"), sem("pv_done"), sem("den_sum")
        den_rcp, o_done = sem("den_rcp"), sem("o_done")
        squares, rms_logged, rms_ready = sem("squares"), sem("rms_logged"), sem("rms_ready")
        o_scaled, y_rounded, y_split = sem("o_scaled"), sem("y_rounded"), sem("y_split")
        wo_rounded, wo_split = sem("wo_rounded"), sem("wo_split")
        res_sum, ln_part, ln_stats = sem("res_sum"), sem("ln_part"), sem("ln_stats")
        ln_logged, ln_rstd_ready, ln_shift_ready = sem("ln_logged"), sem("ln_rstd_ready"), sem("ln_shift_ready")
        normed, gained, finished = sem("normed"), sem("gained"), sem("finished")
        centred, finished_dve = sem("centred"), sem("finished_dve")

        top = -(-nc.sbuf_base // 32) * 32

        def at(name, shape, dt, offset):
            return nc.alloc_sbuf_tensor_at(name, shape, dt, offset=offset)

        class Region:
            def __init__(self, size):
                nonlocal top
                self.base, top = top, top + size
                self.end = top

        def nbytes(*shape):
            return 4 * int(np.prod(shape))

        r_x = Region(2 * nbytes(KT, SEQ))
        lo_half = r_x.base + nbytes(KT, SEQ)
        x_hi = at("x_hi", [P, KT, SEQ], F32R, r_x.base)
        x_lo = at("x_lo", [P, KT, SEQ], F32R, lo_half)
        wo_hi = at("wo_hi", [P, FT, DM], F32R, r_x.base)
        wo_raw = at("wo_raw", [P, FT, DM], F32, lo_half)
        wo_lo = at("wo_lo", [P, FT, DM], F32R, lo_half)
        r_q = Region(nbytes(NB, DM))
        qo = at("qo", [P, NB, DM], F32, r_q.base)
        y_hi = at("y_hi", [P, NB, FT, P], F32R, r_q.base)
        rows = [at(f"rows{s}", [P, DM], F32, r_q.base + s * nbytes(DM)) for s in range(RS)]
        mem_hi = at("mem_hi", [P, KT, MEM], F32R, r_q.base + nbytes(4, DM))
        mem_lo = at("mem_lo", [P, KT, MEM], F32R, r_q.base + nbytes(6, DM))
        k_a = at("k_a", [P, GA, SEQ], F32R, Region(nbytes(GA, SEQ)).base)
        k_b = at("k_b", [P, HB, SEQ], F32R, Region(nbytes(HB, SEQ)).base)
        k_c = at("k_c", [P, HC, MEM], F32R, Region(nbytes(HC, MEM)).base)
        v_a = at("v_a", [P, NB, W_KV], F32, Region(nbytes(NB, W_KV)).base)
        v_b = at("v_b", [P, NB, W_B], F32, Region(nbytes(NB, W_B)).base)
        v_c = at("v_c", [P, NBM, W_C], F32, Region(nbytes(NBM, W_C)).base)
        r_z = Region(nbytes(FT, SEQ))
        zt = at("zt", [P, FT, SEQ], F32, r_z.base)
        y_lo = at("y_lo", [P, FT, SEQ], F32R, r_z.base)
        r_s = Region(4 * nbytes(DM))
        slot = [r_z.base, r_z.base + 2 * nbytes(KT, C), r_s.base]
        w_hi = [at(f"w_hi{s}", [P, KT, C], F32R, o) for s, o in enumerate(slot)]
        w_raw = [at(f"w_raw{s}", [P, KT, C], F32, o + nbytes(KT, C)) for s, o in enumerate(slot)]
        w_lo = [at(f"w_lo{s}", [P, KT, C], F32R, o + nbytes(KT, C)) for s, o in enumerate(slot)]
        gate = [r_s.base + s * 2 * nbytes(KT, P) for s in range(2)]
        g_hi = [at(f"g_hi{s}", [P, KT, P], F32R, o) for s, o in enumerate(gate)]
        g_raw = [at(f"g_raw{s}", [P, KT, P], F32, o + nbytes(KT, P)) for s, o in enumerate(gate)]
        g_lo = [at(f"g_lo{s}", [P, KT, P], F32R, o + nbytes(KT, P)) for s, o in enumerate(gate)]
        gain = at("gain", [P, DM], F32, r_s.base)
        bias = at("bias", [P, DM], F32, r_s.base + nbytes(DM))
        res = [at(f"res{s}", [P, DM], F32, r_s.base + (2 + s) * nbytes(DM)) for s in range(2)]
        r_t = Region(max(nbytes(QKV + 7 * C), nbytes(2 * SEQ + (2 * QS + Q2) * 2 * P)))
        b_row = at("b_row", [P, QKV], F32, r_t.base)
        h_at = r_t.base + nbytes(QKV)
        h_sb = at("h_sb", [P, C], F32, h_at)
        rot_cos = at("rot_cos", [P, C], F32, h_at + nbytes(C))
        rot_sin = at("rot_sin", [P, C], F32, h_at + 2 * nbytes(C))
        keys2 = [at(f"keys2{s}", [P, C // HD, 2, HD], F32, h_at + (3 + 2 * s) * nbytes(C)) for s in range(2)]
        prob = [at(f"prob{s}", [P, SEQ], F32, r_t.base + s * nbytes(SEQ)) for s in range(2)]
        q_at = r_t.base + 2 * nbytes(SEQ)
        q_hi = [at(f"q_hi{s}", [P, 2 * P], F32R, q_at + s * nbytes(2 * P)) for s in range(QS)]
        q_lo = [at(f"q_lo{s}", [P, 2 * P], F32R, q_at + (QS + s) * nbytes(2 * P)) for s in range(QS)]
        r_r = Region(nbytes(NB, 2 * HD))
        q2_at = q_at + 2 * QS * nbytes(2 * P)
        q2 = [at(f"q2{s}", [P, 2, 2, HD], F32, q2_at + s * nbytes(2 * P)) for s in range(Q2)]
        rope = at("rope", [P, NB, 2 * HD], F32, r_r.base)
        gate_e = [at(f"gate_e{s}", [P, HALF], F32, Region(nbytes(HALF)).base) for s in range(2)]
        pt_at = [r_r.base, r_r.base + nbytes(HALF), Region(nbytes(HALF)).base, Region(nbytes(HALF)).base]
        prob_t = [at(f"prob_t{s}", [P, HALF], F32, o) for s, o in enumerate(pt_at)]
        mask_a = at("mask_a", [P, 2 * P], F32, Region(nbytes(2 * P)).base)
        mask_b = at("mask_b", [P, SEQ], F32, Region(nbytes(SEQ)).base)
        ident = at("ident", [P, P], F32, Region(nbytes(P)).base)

        def small(name, *shape):
            return at(name, [P, *shape], F32, Region(-(-nbytes(*shape) // 32) * 32).base)

        z_bias, neg_z_bias = small("z_bias", FT), small("neg_z_bias", FT)
        g_col = small("g_col", FT)
        sink_row, neg_sink = small("sink_row", HA), small("neg_sink", HA)
        mx = small("mx", 2, 2)
        nb = small("nb", 4, 2)
        gap, gap_exp = small("gap", 4, 2), small("gap_exp", 4, 2)
        den, den_all, rden = small("den", 4, 2), small("den_all", 4, 2), small("rden", 4, 2)
        sq = small("sq", 2, 3)
        rms_log, rms = small("rms_log", 2, 3), small("rms", 2, 3)
        square_out = at("square_out", [P, W_A], mybir.dt.bfloat16, Region(2 * W_A).base)
        stats, moments = small("stats", 2, 2, 6), small("moments", 2, 2)
        ln_log, ln_rstd, ln_shift = small("ln_log", 2), small("ln_rstd", 2), small("ln_shift", 2)
        assert top <= nc.sbuf_usable_end, top

        wide = [ctx.enter_context(nc.psum_tensor(f"wide{b}", [P, HALF], F32)) for b in range(3)]
        narrow = [ctx.enter_context(nc.psum_tensor(f"narrow{b}", [P, HALF], F32)) for b in range(2)]
        long_ps = [ctx.enter_context(nc.psum_tensor(f"long_ps{b}", [P, HALF], F32)) for b in range(2)]
        o_ps = ctx.enter_context(nc.psum_tensor("o_ps", [P, HALF], F32))

        def f32(ap):
            return ap.bitcast(F32)

        def bank_of(ring, turns, key):
            n = turns[key]
            return n, ring[n % len(ring)]

        def slot_of(c):
            return (c + 2) % 3

        def heads_view(ap, n):
            return ap.rearrange("p (h d) -> p h d", h=n)

        def key_dst(k):
            c, i = jobs[plan.key_jobs[k]]
            t, n = {"mk": (k_c, HC), "kva": (k_a, GA), "kb": (k_b, HB)}[kinds[c][0]]
            return t[:, :, i * P:(i + 1) * P], n

        def v_tile(u, t, hh):
            kind, _, h0, _, _ = UNITS[u]
            h = h0 + hh
            if kind == "a":
                g = h // (HA // GA)
                return v_a[:, t, g * HD:(g + 1) * HD]
            return (v_b if kind == "b" else v_c)[:, t, h * HD:(h + 1) * HD]

        def q_cols(u, hh):
            kind, _, h0, _, _ = UNITS[u]
            return {"a": 0, "b": W_A, "c": W_A + W_B}[kind] + (h0 + hh) * HD

        a_index = {}
        masked_index = {}
        for u, unit in enumerate(UNITS):
            if unit[0] == "a":
                a_index[u] = len(a_index)
            if unit[0] != "c":
                masked_index[u] = len(masked_index)

        def scores_turn(u):
            return plan.wide["scores", u, len(key_chunks(u)) - 1]

        def probs_turn(u):
            return plan.narrow["probs", u, plan.pt_chunks(u)[-1][0]]

        block = ctx.enter_context(nc.Block())

        @block.sync
        def _(sp):
            def load_rows(r):
                if r >= RS:
                    sp.wait_ge(rows_full, 2 * (r - RS) + 2)
                src = x[0, r * P:(r + 1) * P, :] if r < NB else mem[0, (r - NB) * P:(r - NB + 1) * P, :]
                for h in range(2):
                    cols = slice(h * HALF, (h + 1) * HALF)
                    sp.dma_start(rows[r % RS][:, cols], src[:, cols]).then_inc(rows_in[r % RS][h], 16)

            def load_chunk(c):
                if c >= 3:
                    sp.wait_ge(wide_full, plan.wide["job", plan.last_job[c - 3]] + 1)
                _, of_mem, col, _ = kinds[c]
                src = (w_mem if of_mem else w_in)[0, :, col:col + C]
                src = src.rearrange("(k p) n -> p k n", p=P)
                for h in range(2):
                    k = slice(h * KT // 2, (h + 1) * KT // 2)
                    sp.dma_start(w_raw[slot_of(c)][:, k, :], src[:, k, :])\
                      .then_inc(chunk_in[slot_of(c)][h], 16)

            def load_gate(f):
                if f < 2:
                    sp.wait_ge(wide_full, plan.wide["job", plan.last_job[6]] + 1)
                else:
                    sp.wait_ge(gate_full, 2 * (f - 2) + 2)
                src = w_in[0, :, COL_Z + f * P:COL_Z + (f + 1) * P]
                sp.dma_start(g_raw[f % 2][:, :, :], src.rearrange("(k p) n -> p k n", p=P))\
                  .then_inc(gate_in[f % 2], 16)

            first_cols = slice(COL_KA, COL_KA + C)
            rope_rows = rope_d.rearrange("(b p) d -> p b d", p=P)
            sp.dma_start(ident[:, :], ident_d).then_inc(ident_in, 16)
            load_rows(0)
            load_chunk(0)
            load_rows(1)
            sp.dma_start(b_row[:, first_cols], b_in[0, first_cols].partition_broadcast(P)).then_inc(bias_first_in, 16)
            sp.dma_start(rope[:, 0:2, :], rope_rows[:, 0:2, :]).then_inc(rope_first_in, 16)
            load_rows(2)
            load_rows(3)
            sp.dma_start(rope[:, 2:NB, :], rope_rows[:, 2:NB, :]).then_inc(rope_in, 16)
            load_rows(4)
            load_chunk(1)
            for cols in (slice(0, COL_KA), slice(COL_KA + C, QKV)):
                sp.dma_start(b_row[:, cols], b_in[0, cols].partition_broadcast(P)).then_inc(bias_in, 16)
            for r in range(5, NB + NBM):
                load_rows(r)
            load_chunk(2)
            load_chunk(3)
            with nc.allow_non_contiguous_dma(reason="one value per partition"):
                sp.dma_start(z_bias[:, :], b_in[0, COL_Z:].rearrange("(f p) -> p f", p=P))\
                  .then_inc(gate_cols_in, 16)
                sp.dma_start(g_col[:, :], g_branch[0].rearrange("(f p) -> p f", p=P))\
                  .then_inc(gate_cols_in, 16)
            sp.dma_start(sink_row[:, :], sinks[0].partition_broadcast(P)).then_inc(sinks_in, 16)
            sp.dma_start(mask_a[:, :], mask_a_d).then_inc(masks_in, 16)
            sp.dma_start(mask_b[:, :], mask_b_d).then_inc(masks_in, 16)
            for c in range(4, len(kinds)):
                load_chunk(c)
            for f in range(FT):
                load_gate(f)
            for k in range(FT):
                if k < FT - 1:
                    sp.wait_ge(x_used, k + 1)
                else:
                    sp.wait_ge(gate_full, GATES)
                sp.dma_start(wo_raw[:, k, :], w_out[0, k * P:(k + 1) * P, :]).then_inc(wo_in[k], 16)
            sp.dma_start(gain[:, :], ln_gain[0].partition_broadcast(P)).then_inc(ln_in, 16)
            sp.dma_start(bias[:, :], ln_bias[0].partition_broadcast(P)).then_inc(ln_in, 16)

            def load_residual(i):
                if i >= 2:
                    sp.wait_ge(stored[i % 2], 16 * (i // 2))
                sp.dma_start(res[i % 2][:, :], x[0, i * P:(i + 1) * P, :]).then_inc(res_in[i % 2], 16)

            load_residual(0)
            load_residual(1)
            for i in range(NB):
                if i == NB - 1:
                    sp.wait_ge(finished_dve, 1)
                    sp.dma_start(out[0, i * P:(i + 1) * P, POOL_COLS:], res[i % 2][:, POOL_COLS:])\
                      .then_inc(stored[i % 2], 16)
                    sp.wait_ge(finished, i + 1)
                    sp.dma_start(out[0, i * P:(i + 1) * P, 0:POOL_COLS], res[i % 2][:, 0:POOL_COLS])\
                      .then_inc(stored[i % 2], 16)
                    continue
                sp.wait_ge(finished, i + 1)
                sp.dma_start(out[0, i * P:(i + 1) * P, :], res[i % 2][:, :]).then_inc(stored[i % 2], 16)
                if i + 2 < NB:
                    load_residual(i + 2)
            sp.wait_ge(stored[0], 16 * (NB // 2))
            sp.wait_ge(stored[1], 16 * (NB // 2 + 1))

        @block.tensor
        def _(pe):
            def transpose_rows(r):
                for h in range(2):
                    pe.wait_ge(rows_in[r % RS][h], 16 * (r // RS + 1))
                    if r:
                        pe.wait_ge(rows_split[h], r)
                    for j in range(4):
                        k = 4 * h + j
                        t = pe.transpose(long_ps[h][:, j * P:(j + 1) * P], rows[r % RS][:, k * P:(k + 1) * P],
                                         ident[:, :])
                    t.then_inc(rows_full, 1)

            def project(n):
                c, i = jobs[n]
                of_mem, s = kinds[c][1], slot_of(c)
                r = (NB if of_mem else 0) + i
                _, bank = bank_of(wide, plan.wide, ("job", n))
                if n >= 3:
                    pe.wait_ge(h_read, n - 2)
                t_hi, t_lo = (mem_hi, mem_lo) if of_mem else (x_hi, x_lo)
                cols = slice(i * P, (i + 1) * P)
                for h in range(2):
                    pe.wait_ge(rows_split[h], r + 1)
                    pe.wait_ge(chunk_rounded, 2 * c + h + 1)
                    if c == 0:
                        pe.wait_ge(first_split, h + 1)
                    else:
                        pe.wait_ge(chunk_split, 2 * (c - 1) + h + 1)
                    for k in range(h * KT // 2, (h + 1) * KT // 2):
                        dst = bank[:, 0:C]
                        pe.matmul(dst, t_hi[:, k, cols], w_hi[s][:, k, :], start=(k == 0), stop=False)
                        pe.matmul(dst, t_hi[:, k, cols], w_lo[s][:, k, :], start=False, stop=False)
                        mm = pe.matmul(dst, t_lo[:, k, cols], w_hi[s][:, k, :], start=False, stop=(k == KT - 1))
                mm.then_inc(wide_full, 1)

            def transpose_keys(k):
                _, heads = key_dst(k)
                if k < 2 * NB:
                    pe.wait_ge(keys_rotated, k + 1)
                else:
                    pe.wait_ge(h_read, plan.key_jobs[k] + 1)
                n, bank = bank_of(narrow, plan.narrow, ("keys", k))
                if n >= 2:
                    pe.wait_ge(narrow_read[n % 2], n // 2)
                for h in range(heads):
                    twice = keys2[k % 2][:, h, :, :].rearrange("p a d -> p (a d)")
                    t = pe.transpose(bank[:, h * P:(h + 1) * P], twice, ident[:, :])
                t.then_inc(narrow_full, 1)

            pe.wait_ge(ident_in, 16)
            for what, n in plan.steps:
                {"rows": transpose_rows, "job": project, "keys": transpose_keys}[what](n)

            def last_gate_products(k):
                f = FT - 1
                if k == 0:
                    pe.wait_ge(gate_rounded, f + 1)
                    pe.wait_ge(gate_split, f + 1)
                for h in range(2):
                    if k == 0:
                        pe.wait_ge(gate_done, 2 * f + h - 1)
                    cols = slice(h * HALF, (h + 1) * HALF)
                    dst = long_ps[h][:, :]
                    pe.matmul(dst, g_hi[f % 2][:, k, :], x_hi[:, k, cols], start=(k == 0), stop=False)
                    pe.matmul(dst, g_hi[f % 2][:, k, :], x_lo[:, k, cols], start=False, stop=False)
                    mm = pe.matmul(dst, g_lo[f % 2][:, k, :], x_hi[:, k, cols], start=False, stop=(k == KT - 1))
                    if k == KT - 1:
                        mm.then_inc(gate_full, 1)
                if k < KT - 1:
                    mm.then_inc(x_used, 1)

            def gate_products(v, part):
                n, step = divmod(v, GATE_ITERATIONS)
                f, h = divmod(n, 2)
                shares = 2 * GATE_ITERATIONS
                share = 2 * step + part
                if f == FT - 1:
                    last_gate_products(shares * h + share)
                    return
                if share == 0:
                    pe.wait_ge(gate_rounded, f + 1)
                    pe.wait_ge(gate_split, f + 1)
                    if n >= 2:
                        pe.wait_ge(gate_done, n - 1)
                cols = slice(h * HALF, (h + 1) * HALF)
                dst = long_ps[n % 2][:, :]
                for k in range(share * KT // shares, (share + 1) * KT // shares):
                    pe.matmul(dst, g_hi[f % 2][:, k, :], x_hi[:, k, cols], start=(k == 0), stop=False)
                    pe.matmul(dst, g_hi[f % 2][:, k, :], x_lo[:, k, cols], start=False, stop=False)
                    mm = pe.matmul(dst, g_lo[f % 2][:, k, :], x_hi[:, k, cols], start=False, stop=(k == KT - 1))
                if share == shares - 1:
                    mm.then_inc(gate_full, 1)

            def transpose_q(u):
                heads = UNITS[u][3]
                n, bank = bank_of(narrow, plan.narrow, ("q", u))
                if n >= 2:
                    pe.wait_ge(narrow_read[n % 2], n // 2)
                pe.wait_ge(q_twice, u + 1)
                for hh in range(heads):
                    twice = q2[u % Q2][:, hh, :, :].rearrange("p a d -> p (a d)")
                    t = pe.transpose(bank[:, hh * P:(hh + 1) * P], twice, ident[:, :])
                t.then_inc(narrow_full, 1)

            def score(u):
                kind, i, h0, heads, nk = UNITS[u]
                split = plan.narrow["q", u]
                pe.wait_ge(narrow_read[split % 2], split // 2 + 1)
                if u == 0:
                    pe.wait_ge(h_read, n_jobs)
                    last = plan.narrow["keys", len(plan.key_jobs) - 1]
                    pe.wait_ge(narrow_read[last % 2], last // 2 + 1)
                if u >= 2:
                    pe.wait_ge(probs_ready, u - 1)
                for c, (lo, hi) in enumerate(key_chunks(u)):
                    _, bank = bank_of(wide, plan.wide, ("scores", u, c))
                    for hh in range(heads):
                        h = h0 + hh
                        if kind == "a":
                            dst = bank[:, hh * C:hh * C + nk * P]
                            keys = k_a[:, h // (HA // GA), (i + 1 - nk) * P:(i + 1) * P]
                        elif kind == "b":
                            dst, keys = bank[:, 0:hi - lo], k_b[:, h, lo:hi]
                        else:
                            dst, keys = bank[:, hh * C:(hh + 1) * C], k_c[:, h, :]
                        pe.matmul(dst, q_hi[u % QS][:, hh * P:(hh + 1) * P], keys, start=True, stop=False)
                        mm = pe.matmul(dst, q_lo[u % QS][:, hh * P:(hh + 1) * P], keys, start=False, stop=True)
                    mm.then_inc(wide_full, 1)

            def transpose_probs(u):
                pe.wait_ge(probs_ready, u + 1)
                tiles = prob_tiles(u)
                for c, _ in plan.pt_chunks(u):
                    n, bank = bank_of(narrow, plan.narrow, ("probs", u, c))
                    if n >= 2:
                        pe.wait_ge(narrow_read[n % 2], n // 2)
                    for j, (_, _, col) in enumerate(tiles[4 * c:4 * c + 4]):
                        t = pe.transpose(bank[:, j * P:(j + 1) * P], prob[u % 2][:, col:col + P], ident[:, :])
                    t.then_inc(narrow_full, 1)

            def times_v(u):
                heads = UNITS[u][3]
                for c, _ in plan.pt_chunks(u):
                    n = plan.narrow["probs", u, c]
                    pe.wait_ge(narrow_read[n % 2], n // 2 + 1)
                if u >= 1:
                    pe.wait_ge(o_done, u)
                tiles = prob_tiles(u)
                for hh in range(heads):
                    mine = [(n, t) for n, (h, t, _) in enumerate(tiles) if h == hh]
                    for n, t in mine:
                        w = plan.pt[u, n // 4] % 4
                        mm = pe.matmul(o_ps[:, hh * HD:(hh + 1) * HD],
                                       prob_t[w][:, (n % 4) * P:(n % 4 + 1) * P], v_tile(u, t, hh),
                                       start=(n == mine[0][0]), stop=(n == mine[-1][0]))
                mm.then_inc(pv_done, 1)

            def transpose_y(i, j):
                pe.wait_ge(o_scaled, 3 * i + j + 1)
                n, bank = bank_of(narrow, plan.narrow, ("y", i, j))
                pe.wait_ge(narrow_read[n % 2], n // 2)
                for c, f in enumerate(BRANCH_TILES[j]):
                    t = pe.transpose(bank[:, c * P:(c + 1) * P], qo[:, i, f * P:(f + 1) * P], ident[:, :])
                t.then_inc(narrow_full, 1)

            def out_products(i, v, part):
                order = out_order(i)
                quarters = 4 * OUT_ITERATIONS[i]
                first = 4 * (v - OUT_AT[i]) + part
                end = 4 * (v - OUT_AT[i]) + (1, 4)[part]
                half_done = {half: max(n for n, o in enumerate(order) if o[0] == half) for half in range(2)}
                for n in range(first * len(order) // quarters, end * len(order) // quarters):
                    half, k, p = order[n]
                    j = max(b for b in range(3) if BRANCH_TILES[b][0] <= k)
                    if p == 0 and k == BRANCH_TILES[j][0]:
                        pe.wait_ge(y_split, 3 * i + j + 1)
                    if p == 0 and i == 0 and half == 0:
                        pe.wait_ge(wo_split, k + 1)
                    if p == 0 and k == 0 and i == 0:
                        pe.wait_ge(gate_done, GATES - 1 + half)
                    if p == 0 and k == 0 and i > 0:
                        pe.wait_ge(res_sum, 2 * i + half - 1)
                    y = y_lo[:, k, i * P:(i + 1) * P] if p == 2 else y_hi[:, i, k, :]
                    w = wo_lo if p == 1 else wo_hi
                    mm = pe.matmul(long_ps[half][:, :], y, w[:, k, half * HALF:(half + 1) * HALF],
                                   start=(k == 0 and p == 0), stop=(n == half_done[half]))
                    if n == half_done[half]:
                        mm.then_inc(out_full, 1)

            def filler(v, part):
                if v < GATE_ITERATIONS * GATES:
                    gate_products(v, part)
                for i in range(NB):
                    if OUT_AT[i] <= v < OUT_AT[i] + OUT_ITERATIONS[i]:
                        out_products(i, v, part)

            filler(0, 0)
            transpose_q(0)
            for v in range(ITERATIONS):
                if 0 <= v - 2 < n_units:
                    transpose_probs(v - 2)
                if 0 <= v - 1 < n_units:
                    score(v - 1)
                if v:
                    filler(v, 0)
                for i, j in stage_at(v, Y_AT):
                    transpose_y(i, j)
                filler(v, 1)
                if v + 1 < n_units:
                    transpose_q(v + 1)
                if 0 <= v - 3 < n_units:
                    times_v(v - 3)

        @block.scalar
        def _(act):
            nc.scalar.preload_act_table_set("natural_log_exp_and_others")

            def chunk_hi(c):
                s = slot_of(c)
                for h in range(2):
                    act.wait_ge(chunk_in[s][h], 16 * (c // 3 + 1))
                    k = slice(h * KT // 2, (h + 1) * KT // 2)
                    act.activation(w_hi[s][:, k, :], w_raw[s][:, k, :], ACT.Copy).then_inc(chunk_rounded, 1)

            def rows_hi(r):
                for h in range(2):
                    act.wait_ge(rows_full, 2 * r + h + 1)
                    dst, i = (x_hi, r) if r < NB else (mem_hi, r - NB)
                    act.activation(dst[:, 4 * h:4 * h + 4, i * P:(i + 1) * P],
                                   long_ps[h][:, :].rearrange("p (k t) -> p k t", k=4), ACT.Copy)\
                       .then_inc(rows_rounded, 1)

            def keys_hi(k):
                dst, heads = key_dst(k)
                act.wait_ge(narrow_full, plan.narrow["keys", k] + 1)
                _, bank = bank_of(narrow, plan.narrow, ("keys", k))
                act.activation(dst, bank[:, 0:heads * P].rearrange("p (h t) -> p h t", h=heads), ACT.Copy)\
                   .then_inc(keys_rounded, 1)

            def gate_hi(f):
                act.wait_ge(gate_in[f % 2], 16 * (f // 2 + 1))
                act.activation(g_hi[f % 2][:, :, :], g_raw[f % 2][:, :, :], ACT.Copy).then_inc(gate_rounded, 1)

            split_at = {c: plan.last_job[c - 1] - 3 for c in range(1, len(kinds))}
            split_at[5] = plan.last_job[3]
            rows_hi(0)
            chunk_hi(0)
            for what, n in plan.steps[1:]:
                if what == "rows":
                    rows_hi(n)
                elif what == "keys":
                    keys_hi(n)
                else:
                    for c, job in split_at.items():
                        if job == n:
                            chunk_hi(c)
                    if n == n_jobs - 4:
                        gate_hi(0)
                    if n == n_jobs - 3:
                        gate_hi(1)

            def half_sigmoid(n):
                e = gate_e[n % 2][:, :]
                if n >= 2:
                    act.wait_ge(gate_done, n - 1)
                act.wait_ge(gate_full, n + 1)
                act.activation(e, long_ps[n % 2][:, :], ACT.Exp, bias=neg_z_bias[:, n // 2:n // 2 + 1], scale=-1.0)\
                   .then_inc(gate_exp, 1)
                act.wait_ge(gate_exp, n + 1)
                act.activation(e, e, ACT.Ln, bias=1.0).then_inc(gate_logged, 1)
                act.wait_ge(gate_logged, n + 1)
                act.activation(e, e, ACT.Exp, scale=-1.0).then_inc(gate_sigmoid, 1)

            def unit_q_hi(u):
                heads = UNITS[u][3]
                act.wait_ge(narrow_full, plan.narrow["q", u] + 1)
                _, bank = bank_of(narrow, plan.narrow, ("q", u))
                if u >= QS:
                    act.wait_ge(wide_full, scores_turn(u - QS) + 1)
                act.activation(q_hi[u % QS][:, 0:heads * P], bank[:, 0:heads * P], ACT.Copy, scale=SCALE)\
                   .then_inc(q_rounded, 1)

            def unit_exp(u):
                kind, _, _, heads, nk = UNITS[u]
                s, r = u % 2, u % 4
                act.wait_ge(neg_max, u + 1)
                if kind == "c":
                    _, bank = bank_of(wide, plan.wide, ("scores", u, 0))
                    if u >= 2:
                        act.wait_ge(narrow_full, probs_turn(u - 2) + 1)
                if u >= 4:
                    act.wait_ge(o_done, u - 3)
                for hh in range(heads):
                    cols = slice(hh * C, hh * C + nk * P)
                    src = bank[:, cols] if kind == "c" else prob[s][:, cols]
                    e = act.activation(prob[s][:, cols], src, ACT.Exp, bias=nb[:, r, hh:hh + 1],
                                       accum_out=den[:, r, hh:hh + 1])
                e.then_inc(probs_ready, 1)
                if kind == "a":
                    act.wait_ge(sink_gap_ready, a_index[u] + 1)
                    act.activation(gap_exp[:, r, :], gap[:, r, :], ACT.Exp).then_inc(sink_exp_ready, 1)

            def unit_pt(u):
                for c, w in plan.pt_chunks(u):
                    act.wait_ge(narrow_full, plan.narrow["probs", u, c] + 1)
                    n, bank = bank_of(narrow, plan.narrow, ("probs", u, c))
                    if w >= 4:
                        act.wait_ge(pv_done, plan.pt_unit[w - 4] + 1)
                    size = P * len(prob_tiles(u)[4 * c:4 * c + 4])
                    act.activation(prob_t[w % 4][:, 0:size], bank[:, 0:size], ACT.Copy).then_inc(narrow_read[n % 2], 1)

            def branch_rms(i, j):
                lo, n = BRANCHES[j]
                act.wait_ge(o_done, branch_done(i, j) - 3)
                act.activation(square_out[:, 0:n], qo[:, i, lo:lo + n], ACT.Square, scale=float(n) ** -0.5,
                               accum_out=sq[:, i % 2, j:j + 1]).then_inc(squares, 1)
                act.wait_ge(squares, 3 * i + j + 1)
                act.activation(rms_log[:, i % 2, j:j + 1], sq[:, i % 2, j:j + 1], ACT.Ln, bias=RMS_EPS)\
                   .then_inc(rms_logged, 1)
                act.wait_ge(rms_logged, 3 * i + j + 1)
                act.activation(rms[:, i % 2, j:j + 1], rms_log[:, i % 2, j:j + 1], ACT.Exp, scale=-0.5)\
                   .then_inc(rms_ready, 1)

            act.wait_ge(negated, 2)
            unit_q_hi(0)
            for v in range(ITERATIONS):
                for k in wo_tiles(v):
                    act.wait_ge(wo_in[k], 16)
                    act.activation(wo_hi[:, k, :], wo_raw[:, k, :], ACT.Copy, scale=g_col[:, k:k + 1])\
                       .then_inc(wo_rounded, 1)
                if 0 <= v - 2 < n_units:
                    unit_pt(v - 2)
                if 0 <= v - 1 < n_units:
                    unit_exp(v - 1)
                if v + 1 < n_units:
                    unit_q_hi(v + 1)
                f, since = divmod(v, 2 * GATE_ITERATIONS)
                if since == GATE_ITERATIONS and 1 <= f < FT - 1:
                    gate_hi(f + 1)
                for n in halves_at(v):
                    half_sigmoid(n)
                for i in stage_at(v, NORM_AT):
                    s = i % 2
                    cols = slice(0, DM if i < NB - 1 else POOL_COLS)
                    act.wait_ge(ln_shift_ready, i + 1)
                    act.activation(res[s][:, cols], res[s][:, cols], ACT.Identity, bias=ln_shift[:, s:s + 1],
                                   scale=ln_rstd[:, s:s + 1]).then_inc(normed, 1)
                for i, j in stage_at(v, RMS_AT):
                    branch_rms(i, j)
                for i, j in stage_at(v, YSPLIT_AT):
                    n = plan.narrow["y", i, j]
                    act.wait_ge(narrow_read[n % 2], n // 2 + 1)
                    f = slice(BRANCH_TILES[j][0], BRANCH_TILES[j][-1] + 1)
                    act.activation(y_hi[:, i, f, :], zt[:, f, i * P:(i + 1) * P], ACT.Copy).then_inc(y_rounded, 1)
                for i in stage_at(v, STATS_AT):
                    s = i % 2
                    act.wait_ge(ln_stats, i + 1)
                    act.activation(ln_log[:, s:s + 1], moments[:, s, 1:2], ACT.Ln, bias=LN_EPS).then_inc(ln_logged, 1)
                    act.wait_ge(ln_logged, i + 1)
                    act.activation(ln_rstd[:, s:s + 1], ln_log[:, s:s + 1], ACT.Exp, scale=-0.5)\
                       .then_inc(ln_rstd_ready, 1)

        @block.vector
        def _(dve):
            def rows_lo(r):
                for h in range(2):
                    dve.wait_ge(rows_rounded, 2 * r + h + 1)
                    hi, lo, i = (x_hi, x_lo, r) if r < NB else (mem_hi, mem_lo, r - NB)
                    ks, cols = slice(4 * h, 4 * h + 4), slice(i * P, (i + 1) * P)
                    dve.tensor_tensor(lo[:, ks, cols], long_ps[h][:, :].rearrange("p (k t) -> p k t", k=4),
                                      f32(hi[:, ks, cols]), ALU.subtract).then_inc(rows_split[h], 1)

            def keys_lo(k):
                dst, heads = key_dst(k)
                dve.wait_ge(keys_rounded, k + 1)
                n, bank = bank_of(narrow, plan.narrow, ("keys", k))
                dve.tensor_tensor(dst[HD:P], bank[HD:P, 0:heads * P].rearrange("p (h t) -> p h t", h=heads),
                                  f32(dst[HD:P]), ALU.subtract).then_inc(narrow_read[n % 2], 1)

            rotations = [0]

            def finish_job(n):
                c, i = jobs[n]
                kind, of_mem, col, q_col = kinds[c]
                dve.wait_ge(wide_full, plan.wide["job", n] + 1)
                _, bank = bank_of(wide, plan.wide, ("job", n))
                if n == 0:
                    dve.wait_ge(bias_first_in, 16)
                    dve.wait_ge(rope_first_in, 16)
                if n == 2:
                    dve.wait_ge(rope_in, 16)
                if n == NB:
                    dve.wait_ge(bias_in, 32)
                k = plan.key_jobs.index(n) if n in plan.key_jobs else None
                if k is not None and k >= 2:
                    dve.wait_ge(narrow_full, plan.narrow["keys", k - 2] + 1)
                if kind == "mk":
                    dve.tensor_copy(keys2[k % 2][:, :, :, :],
                                    heads_view(bank[:, 0:C], HC).unsqueeze(2).to_broadcast([P, HC, 2, HD]))\
                       .then_inc(h_read, 1)
                elif kind == "mv":
                    dve.tensor_copy(v_c[:, i, :], bank[:, 0:C]).then_inc(h_read, 1)
                else:
                    b = b_row[:, col:col + C]
                    dst = {"vb": v_b[:, i, :], "qc": qo[:, i, q_col:q_col + C] if q_col is not None else None}\
                        .get(kind, h_sb[:, :])
                    if kind == "kva":
                        dve.tensor_tensor(v_a[:, i, :], bank[:, W_KV:C], b[:, W_KV:C], ALU.add)
                        dst, b = h_sb[:, 0:W_KV], b[:, 0:W_KV]
                    dve.tensor_tensor(dst, bank[:, 0:b.shape[1]], b, ALU.add).then_inc(h_read, 1)
                if kind in ("kva", "kb", "q"):
                    m = rotations[0]
                    rotations[0] += 1
                    width = W_KV if kind == "kva" else C
                    nh = width // HD
                    dve.wait_ge(h_read, n + 1)
                    h3 = heads_view(h_sb[:, 0:width], nh)
                    r3, s3 = heads_view(rot_cos[:, 0:width], nh), heads_view(rot_sin[:, 0:width], nh)
                    tab = rope[:, i, :]

                    def per_head(lo, hi):
                        return tab[:, lo:hi].unsqueeze(1).to_broadcast([P, nh, hi - lo])

                    half = HD // 2
                    dve.tensor_tensor(r3, h3, per_head(0, HD), ALU.mult)
                    dve.tensor_tensor(s3[:, :, 0:half], h3[:, :, half:HD], per_head(HD, HD + half), ALU.mult)
                    dve.tensor_tensor(s3[:, :, half:HD], h3[:, :, 0:half], per_head(HD + half, 2 * HD), ALU.mult)\
                       .then_inc(rope_parts, 1)
                    dve.wait_ge(rope_parts, m + 1)
                    if k is not None:
                        shape = [P, nh, 2, HD]
                        dve.tensor_tensor(keys2[k % 2][:, 0:nh, :, :], r3.unsqueeze(2).to_broadcast(shape),
                                          s3.unsqueeze(2).to_broadcast(shape), ALU.add).then_inc(keys_rotated, 1)
                    else:
                        dve.tensor_tensor(qo[:, i, q_col:q_col + C], rot_cos[:, :], rot_sin[:, :], ALU.add)\
                           .then_inc(q_rotated, 1)

            rows_lo(0)
            for h in range(2):
                s = slot_of(0)
                k = slice(h * KT // 2, (h + 1) * KT // 2)
                dve.wait_ge(chunk_rounded, h + 1)
                dve.tensor_tensor(w_lo[s][:, k, :], w_raw[s][:, k, :], f32(w_hi[s][:, k, :]), ALU.subtract)\
                   .then_inc(first_split, 1)
            for what, n in plan.steps[1:]:
                {"rows": rows_lo, "job": finish_job, "keys": keys_lo}[what](n)

            dve.wait_ge(gate_cols_in, 32)
            dve.wait_ge(sinks_in, 16)
            dve.tensor_scalar(neg_z_bias[:, :], z_bias[:, :], -1.0, None, ALU.mult).then_inc(negated, 1)
            dve.tensor_scalar(neg_sink[:, :], sink_row[:, :], -1.0, None, ALU.mult).then_inc(negated, 1)

            def half_silu(n):
                f, h = divmod(n, 2)
                dve.wait_ge(gate_sigmoid, n + 1)
                dve.scalar_tensor_tensor(zt[:, f, h * HALF:(h + 1) * HALF], long_ps[n % 2][:, :], z_bias[:, f:f + 1],
                                         gate_e[n % 2][:, :], ALU.add, ALU.mult).then_inc(gate_done, 1)

            def unit_q_lo(u):
                heads = UNITS[u][3]
                dve.wait_ge(q_rounded, u + 1)
                n, bank = bank_of(narrow, plan.narrow, ("q", u))
                if u >= QS:
                    dve.wait_ge(wide_full, scores_turn(u - QS) + 1)
                dve.scalar_tensor_tensor(q_lo[u % QS][:, 0:heads * P], bank[:, 0:heads * P], SCALE,
                                         f32(q_hi[u % QS][:, 0:heads * P]), ALU.mult, ALU.subtract)\
                   .then_inc(narrow_read[n % 2], 1)

            def unit_max(u):
                kind, i, h0, heads, nk = UNITS[u]
                s, r = u % 2, u % 4
                if u >= 4:
                    dve.wait_ge(probs_ready, u - 3)
                if kind == "c":
                    dve.wait_ge(wide_full, plan.wide["scores", u, 0] + 1)
                    _, bank = bank_of(wide, plan.wide, ("scores", u, 0))
                    dve.tensor_reduce(nb[:, r, :], heads_view(bank[:, 0:2 * C], 2), AX.X, ALU.max, negate=True)\
                       .then_inc(neg_max, 1)
                    return
                if u >= 2:
                    dve.wait_ge(narrow_full, probs_turn(u - 2) + 1)
                for c, (lo, hi) in enumerate(key_chunks(u)):
                    dve.wait_ge(wide_full, plan.wide["scores", u, c] + 1)
                    _, bank = bank_of(wide, plan.wide, ("scores", u, c))
                    if kind == "b":
                        off = (NB - nk) * P
                        ttr = dve.tensor_tensor_reduce(prob[s][:, lo:hi], bank[:, 0:hi - lo],
                                                       mask_b[:, off + lo:off + hi], 1.0, -3e38, ALU.add, ALU.max,
                                                       mx[:, s, c:c + 1])
                    else:
                        for hh in range(heads):
                            cols = slice(hh * C, hh * C + nk * P)
                            ttr = dve.tensor_tensor_reduce(prob[s][:, cols], bank[:, cols],
                                                           mask_a[:, (2 - nk) * P:2 * P], 1.0, -3e38, ALU.add,
                                                           ALU.max, mx[:, s, hh:hh + 1])
                ttr.then_inc(row_max, 1)
                dve.wait_ge(row_max, masked_index[u] + 1)
                if kind == "b":
                    dve.tensor_reduce(nb[:, r, 0:1], mx[:, s, 0:len(key_chunks(u))], AX.X, ALU.max, negate=True)\
                       .then_inc(neg_max, 1)
                else:
                    ns = neg_sink[:, h0:h0 + 2]
                    dve.scalar_tensor_tensor(nb[:, r, :], mx[:, s, :], -1.0, ns, ALU.mult, ALU.min)\
                       .then_inc(neg_max, 1)
                    dve.wait_ge(neg_max, u + 1)
                    dve.tensor_tensor(gap[:, r, :], nb[:, r, :], ns, ALU.subtract).then_inc(sink_gap_ready, 1)

            def unit_out(u):
                kind, i, _, heads, _ = UNITS[u]
                r = u % 4
                dve.wait_ge(probs_ready, u + 1)
                total = den
                if kind == "a":
                    dve.wait_ge(sink_exp_ready, a_index[u] + 1)
                    dve.tensor_tensor(den_all[:, r, :], den[:, r, :], gap_exp[:, r, :], ALU.add)\
                       .then_inc(den_sum, 1)
                    dve.wait_ge(den_sum, a_index[u] + 1)
                    total = den_all
                dve.reciprocal(rden[:, r, 0:heads], total[:, r, 0:heads]).then_inc(den_rcp, 1)
                dve.wait_ge(den_rcp, u + 1)
                dve.wait_ge(pv_done, u + 1)
                col = q_cols(u, 0)
                dve.tensor_tensor(heads_view(qo[:, i, col:col + heads * HD], heads),
                                  heads_view(o_ps[:, 0:heads * HD], heads),
                                  rden[:, r, 0:heads].unsqueeze(2).to_broadcast([P, heads, HD]), ALU.mult)\
                   .then_inc(o_done, 1)

            dve.wait_ge(negated, 2)
            dve.wait_ge(masks_in, 32)
            unit_q_lo(0)
            for v in range(ITERATIONS):
                if 0 <= v - 4 < n_units:
                    unit_out(v - 4)
                if 0 <= v - 1 < n_units:
                    unit_max(v - 1)
                for n in halves_at(v - 1):
                    half_silu(n)
                for i, j in stage_at(v, Y_AT):
                    n, bank = bank_of(narrow, plan.narrow, ("y", i, j))
                    dve.wait_ge(narrow_full, n + 1)
                    tiles = len(BRANCH_TILES[j])
                    z = zt[:, BRANCH_TILES[j][0]:BRANCH_TILES[j][-1] + 1, i * P:(i + 1) * P]
                    dve.tensor_tensor(z, bank[:, 0:tiles * P].rearrange("p (f t) -> p f t", f=tiles), z, ALU.mult)\
                       .then_inc(narrow_read[n % 2], 1)
                for i in stage_at(v, NORM_AT):
                    s = i % 2
                    dve.wait_ge(ln_rstd_ready, i + 1)
                    dve.scalar_tensor_tensor(ln_shift[:, s:s + 1], moments[:, s, 0:1], -1.0, ln_rstd[:, s:s + 1],
                                             ALU.mult, ALU.mult).then_inc(ln_shift_ready, 1)
                    if i == NB - 1:
                        cols = slice(POOL_COLS, DM)
                        dve.wait_ge(ln_in, 32)
                        dve.scalar_tensor_tensor(res[s][:, cols], res[s][:, cols], moments[:, s, 0:1], gain[:, cols],
                                                 ALU.subtract, ALU.mult).then_inc(centred, 1)
                        dve.wait_ge(centred, 1)
                        dve.scalar_tensor_tensor(res[s][:, cols], res[s][:, cols], ln_rstd[:, s:s + 1], bias[:, cols],
                                                 ALU.mult, ALU.add).then_inc(finished_dve, 1)
                for half in range(2):
                    for i in stage_at(v, RES_AT[half]):
                        cols = slice(half * HALF, (half + 1) * HALF)
                        dve.wait_ge(res_in[i % 2], 16 * (i // 2 + 1))
                        dve.wait_ge(out_full, 2 * i + half + 1)
                        dve.scalar_tensor_tensor(res[i % 2][:, cols], res[i % 2][:, cols], ALPHA, long_ps[half][:, :],
                                                 ALU.mult, ALU.add).then_inc(res_sum, 1)
                        dve.wait_ge(res_sum, 2 * i + half + 1)
                        dve.bn_stats(stats[:, i % 2, half, :], res[i % 2][:, cols]).then_inc(ln_part, 1)
                for k in wo_tiles(v):
                    dve.wait_ge(wo_rounded, k + 1)
                    dve.scalar_tensor_tensor(wo_lo[:, k, :], wo_raw[:, k, :], g_col[:, k:k + 1], f32(wo_hi[:, k, :]),
                                             ALU.mult, ALU.subtract).then_inc(wo_split, 1)
                for i, j in stage_at(v, SCALE_AT):
                    lo, n = BRANCHES[j]
                    dve.wait_ge(rms_ready, 3 * i + j + 1)
                    dve.tensor_scalar(qo[:, i, lo:lo + n], qo[:, i, lo:lo + n], rms[:, i % 2, j:j + 1], None,
                                      ALU.mult).then_inc(o_scaled, 1)
                if v + 1 < n_units:
                    unit_q_lo(v + 1)
                for i in stage_at(v, STATS_AT):
                    dve.wait_ge(ln_part, 2 * i + 2)
                    dve.bn_aggr(moments[:, i % 2, :], stats[:, i % 2, :, :]).then_inc(ln_stats, 1)

        @block.gpsimd
        def _(pool):
            for c in range(1, len(kinds)):
                s = slot_of(c)
                for h in range(2):
                    pool.wait_ge(chunk_rounded, 2 * c + h + 1)
                    k = slice(h * KT // 2, (h + 1) * KT // 2)
                    pool.tensor_tensor(w_lo[s][:, k, :], w_raw[s][:, k, :], f32(w_hi[s][:, k, :]), ALU.subtract)\
                        .then_inc(chunk_split, 1)

            def gate_lo(f):
                pool.wait_ge(gate_rounded, f + 1)
                pool.tensor_tensor(g_lo[f % 2][:, :, :], g_raw[f % 2][:, :, :], f32(g_hi[f % 2][:, :, :]),
                                   ALU.subtract).then_inc(gate_split, 1)

            gate_lo(0)
            gate_lo(1)

            def unit_q_twice(u):
                _, i, _, heads, _ = UNITS[u]
                if u >= Q2:
                    pool.wait_ge(narrow_full, plan.narrow["q", u - Q2] + 1)
                q = heads_view(qo[:, i, q_cols(u, 0):q_cols(u, 0) + heads * HD], heads)
                pool.tensor_copy(q2[u % Q2][:, 0:heads, :, :], q.unsqueeze(2).to_broadcast([P, heads, 2, HD]))\
                    .then_inc(q_twice, 1)

            pool.wait_ge(q_rotated, 3 * NB)
            pool.wait_ge(h_read, n_jobs)
            for u in range(Q2 - 1):
                unit_q_twice(u)
            for v in range(ITERATIONS):
                if v + Q2 - 1 < n_units:
                    unit_q_twice(v + Q2 - 1)
                for i, j in stage_at(v, YSPLIT_AT):
                    pool.wait_ge(y_rounded, 3 * i + j + 1)
                    f, cols = slice(BRANCH_TILES[j][0], BRANCH_TILES[j][-1] + 1), slice(i * P, (i + 1) * P)
                    pool.tensor_tensor(y_lo[:, f, cols], zt[:, f, cols], f32(y_hi[:, i, f, :]), ALU.subtract)\
                        .then_inc(y_split, 1)
                for i in stage_at(v, NORM_AT):
                    s = i % 2
                    cols = slice(0, DM if i < NB - 1 else POOL_COLS)
                    if i == 0:
                        pool.wait_ge(ln_in, 32)
                    pool.wait_ge(normed, i + 1)
                    pool.tensor_tensor(res[s][:, cols], res[s][:, cols], gain[:, cols], ALU.mult).then_inc(gained, 1)
                    pool.wait_ge(gained, i + 1)
                    pool.tensor_tensor(res[s][:, cols], res[s][:, cols], bias[:, cols], ALU.add).then_inc(finished, 1)
                f, since = divmod(v, 2 * GATE_ITERATIONS)
                if since == GATE_ITERATIONS and 1 <= f < FT - 1:
                    gate_lo(f + 1)


def rope_table():
    pos = np.arange(SEQ, dtype=np.float32)
    inv = np.float32(10000.0) ** (-np.arange(0, HD, 2, dtype=np.float32) / np.float32(HD))
    ang = pos[:, None] * inv[None, :].astype(np.float32)
    c, s = np.cos(ang), np.sin(ang)
    return np.concatenate([c, c, -s, s], axis=1).astype(np.float32)


def masks():
    p = np.arange(P)[:, None]
    d = p + P - np.arange(2 * P)[None, :]
    a = np.where((d >= 0) & (d < WINDOW), 0.0, MASKED).astype(np.float32)
    d = p + (NB - 1) * P - np.arange(SEQ)[None, :]
    count = sum(((d >= 0) & (d <= w) & (d % r == 0)).astype(np.float64) for w, r in PAIRS)
    b = np.where(count > 0, np.log(np.maximum(count, 1.0)), MASKED).astype(np.float32)
    return a, b


_INS = ["x", "mem", "w_in", "b_in", "w_mem", "attn_sinks", "g_branch", "w_out", "ln_gain", "ln_bias"]


def kernel(**inputs):
    import concourse.bacc as bacc
    from concourse.bass_utils import run_bass_kernel_spmd

    nc = bacc.Bacc("TRN2", target_bir_lowering=False, num_devices=1, dynamic_dma_scratch_size=1024)
    mask_a, mask_b = masks()
    arrays = {name: np.ascontiguousarray(inputs[name]) for name in _INS}
    arrays |= {"ident": np.eye(P, dtype=np.float32), "rope": rope_table(), "mask_a": mask_a, "mask_b": mask_b}
    arrays = {f"in_{name}": a for name, a in arrays.items()}
    args = [nc.dram_tensor(name, a.shape, mybir.dt.from_np(a.dtype), kind="ExternalInput").ap()
            for name, a in arrays.items()]
    out = nc.dram_tensor("out", (1, SEQ, DM), F32, kind="ExternalOutput").ap()
    layer(nc, *args, out)
    r = run_bass_kernel_spmd(nc, [arrays], core_ids=[0])
    return r.results[0]["out"]
```
